# Optimizing a Trainium2 kernel written in Bass

```python
import math
import jax, jax.numpy as jnp
from jax import lax
import numpy as np
import jax
import jax.numpy as jnp

D_MODEL = 1024
BATCH = 1
SEQ = 512
DEPTH = 1

CTX_LEN = 256
GRID_W = 64
N_MIXERS = 3
CHUNK = 64
Q_BLOCK = 128
EPS = 1e-6

GDN_HEADS = 8
GDN_DK = D_MODEL // GDN_HEADS
GDN_DV = D_MODEL // GDN_HEADS
GDN_CONV = 5
GDN_IN = 2 * GDN_HEADS * GDN_DK + 2 * GDN_HEADS * GDN_DV + 4 * GDN_HEADS

MLSTM_HEADS = 8
MLSTM_DQK = D_MODEL // (2 * MLSTM_HEADS)
MLSTM_DV = D_MODEL // MLSTM_HEADS
MLSTM_IN = 2 * MLSTM_HEADS * MLSTM_DQK + 2 * MLSTM_HEADS * MLSTM_DV + 4 * MLSTM_HEADS

ATTN_HEADS = 8
ATTN_KV_HEADS = 2
ATTN_GROUP = ATTN_HEADS // ATTN_KV_HEADS
ATTN_DH = D_MODEL // ATTN_HEADS
ATTN_IN = (ATTN_HEADS + 2 * ATTN_KV_HEADS) * ATTN_DH
ROPE_THETA = 10000.0

FFN_DIM = ((8 * D_MODEL // 3 + 127) // 128) * 128
FFN_CONV = 3


F32 = jnp.float32

def rms_norm(x, g):
    xf = x.astype(F32)
    y = xf * lax.rsqrt(jnp.mean(xf * xf, axis=-1, keepdims=True) + EPS)
    return (y * g.astype(F32)).astype(x.dtype)

def l2_norm(x):
    xf = x.astype(F32)
    return xf * lax.rsqrt(jnp.sum(xf * xf, axis=-1, keepdims=True) + EPS)

def modulate(h, shift, scale):
    return h * (1.0 + scale) + shift

def dw_conv(x, w):
    k = w.shape[0]
    return lax.conv_general_dilated(
        x, w[:, None, :].astype(x.dtype), window_strides=(1,), padding=[(k // 2, k // 2)],
        dimension_numbers=("NWC", "WIO", "NWC"), feature_group_count=x.shape[-1])

def to_chunks(t):
    b, l, h = t.shape[:3]
    t = t.reshape(b, l // CHUNK, CHUNK, h, *t.shape[3:])
    return jnp.moveaxis(t, (1, 3), (0, 2))

def from_chunks(t):
    t = jnp.moveaxis(t, (0, 2), (1, 3))
    return t.reshape(t.shape[0], t.shape[1] * t.shape[2], *t.shape[3:])

def tri_masks():
    i = jnp.arange(CHUNK)
    return i[:, None] >= i[None, :], i[:, None] > i[None, :]

def flip_seq(t):
    return jnp.flip(t, axis=1)

def identity(t):
    return t

def gated_delta_chunked(q, k, v, beta, g, s0):
    incl, strict = tri_masks()
    q, k, v, beta, g = map(to_chunks, (q, k, v, beta, g))
    gc = jnp.cumsum(g, axis=-1)
    decay = jnp.exp(jnp.where(incl, gc[..., :, None] - gc[..., None, :], -jnp.inf))
    kk = jnp.einsum("nbhid,nbhjd->nbhij", k, k)
    a_mat = jnp.where(strict, beta[..., :, None] * kk * decay, 0.0) + jnp.eye(CHUNK, dtype=kk.dtype)
    rhs = jnp.concatenate([v * beta[..., None], k * (beta * jnp.exp(gc))[..., None]], axis=-1)
    sol = lax.linalg.triangular_solve(a_mat, rhs, left_side=True, lower=True, unit_diagonal=True)
    dv = v.shape[-1]
    u, w = sol[..., :dv], sol[..., dv:]
    qk = jnp.einsum("nbhid,nbhjd->nbhij", q, k) * decay
    q_dec = q * jnp.exp(gc)[..., None]
    k_dec = k * jnp.exp(gc[..., -1:] - gc)[..., None]
    a_last = jnp.exp(gc[..., -1])

    def step(s, xs):
        qd, kd, u_c, w_c, qk_c, al = xs
        v_new = u_c - jnp.einsum("bhck,bhkv->bhcv", w_c, s)
        o = jnp.einsum("bhck,bhkv->bhcv", qd, s) + jnp.einsum("bhij,bhjv->bhiv", qk_c, v_new)
        s = s * al[..., None, None] + jnp.einsum("bhck,bhcv->bhkv", kd, v_new)
        return s, o

    s_fin, o = lax.scan(step, s0, (q_dec, k_dec, u, w, qk, a_last))
    return from_chunks(o), s_fin

def gdn_project(h, w_in, conv_w, a_log, dt_bias):
    bsz, l, _ = h.shape
    nqk, nv = GDN_HEADS * GDN_DK, GDN_HEADS * GDN_DV
    z = h @ w_in
    qkv = jax.nn.silu(dw_conv(z[..., :2 * nqk + nv], conv_w))
    q = l2_norm(qkv[..., :nqk].reshape(bsz, l, GDN_HEADS, GDN_DK)) * (GDN_DK ** -0.5)
    k = l2_norm(qkv[..., nqk:2 * nqk].reshape(bsz, l, GDN_HEADS, GDN_DK))
    v = qkv[..., 2 * nqk:].reshape(bsz, l, GDN_HEADS, GDN_DV).astype(F32)
    gate = z[..., 2 * nqk + nv:2 * nqk + 2 * nv]
    ba = z[..., 2 * nqk + 2 * nv:].reshape(bsz, l, 2, 2, GDN_HEADS).astype(F32)
    beta = jax.nn.sigmoid(ba[:, :, :, 0])
    g = -jnp.exp(a_log.astype(F32)) * jax.nn.softplus(ba[:, :, :, 1] + dt_bias.astype(F32))
    return q, k, v, beta, g, gate

def gdn_mixer(h_ctx, h_lat, want_ctx, w_in, conv_w, a_log, dt_bias, norm_g, w_out):
    qc, kc, vc, bc, gcx, gate_c = gdn_project(h_ctx, w_in, conv_w, a_log, dt_bias)
    ql, kl, vl, bl, glt, gate_l = gdn_project(h_lat, w_in, conv_w, a_log, dt_bias)
    s0 = jnp.zeros((h_ctx.shape[0], GDN_HEADS, GDN_DK, GDN_DV), F32)
    o_ctx, o_lat = [], []
    for d, f in enumerate((identity, flip_seq)):
        oc, s_ctx = gated_delta_chunked(f(qc), f(kc), f(vc), f(bc[:, :, d]), f(gcx[:, :, d]), s0)
        ol, _ = gated_delta_chunked(f(ql), f(kl), f(vl), f(bl[:, :, d]), f(glt[:, :, d]), s_ctx)
        o_ctx.append(f(oc))
        o_lat.append(f(ol))

    def finish(o_pair, gate, dtype):
        o = rms_norm(o_pair[0] + o_pair[1], norm_g)
        o = o.reshape(*o.shape[:2], GDN_HEADS * GDN_DV) * jax.nn.silu(gate.astype(F32))
        return o.astype(dtype) @ w_out

    y_ctx = finish(o_ctx, gate_c, h_ctx.dtype) if want_ctx else None
    return y_ctx, finish(o_lat, gate_l, h_lat.dtype)

def mlstm_chunked(q, k, v, ig, lf, c0, n0, m0):
    incl, _ = tri_masks()
    q, k, v, ig, lf = map(to_chunks, (q, k, v, ig, lf))
    b = jnp.cumsum(lf, axis=-1)
    dlog = jnp.where(incl, b[..., :, None] - b[..., None, :] + ig[..., None, :], -jnp.inf)
    a = jnp.max(dlog, axis=-1)
    p = jnp.exp(dlog - a[..., None]) * jnp.einsum("nbhid,nbhjd->nbhij", q, k)
    num_in = jnp.einsum("nbhij,nbhjv->nbhiv", p, v)
    den_in = jnp.sum(p, axis=-1)
    b_last = b[..., -1]
    wlog = b_last[..., None] - b + ig
    m_loc = jnp.max(wlog, axis=-1)
    kw = k * jnp.exp(wlog - m_loc[..., None])[..., None]
    dc = jnp.einsum("nbhck,nbhcv->nbhkv", kw, v)
    dn = jnp.sum(kw, axis=-2)

    def step(carry, xs):
        cm, nm, mm = carry
        qc, bc, ac, num_c, den_c, bl, ml, dcc, dnc = xs
        m_t = jnp.maximum(ac, bc + mm[..., None])
        s_inter = jnp.exp(bc + mm[..., None] - m_t)
        s_intra = jnp.exp(ac - m_t)
        num = s_inter[..., None] * jnp.einsum("bhck,bhkv->bhcv", qc, cm) + s_intra[..., None] * num_c
        den = s_inter * jnp.einsum("bhck,bhk->bhc", qc, nm) + s_intra * den_c
        h = num / jnp.maximum(jnp.abs(den), jnp.exp(-m_t))[..., None]
        m_new = jnp.maximum(bl + mm, ml)
        f_sc = jnp.exp(bl + mm - m_new)
        i_sc = jnp.exp(ml - m_new)
        cm = f_sc[..., None, None] * cm + i_sc[..., None, None] * dcc
        nm = f_sc[..., None] * nm + i_sc[..., None] * dnc
        return (cm, nm, m_new), h

    (c_f, n_f, m_f), h = lax.scan(step, (c0, n0, m0), (q, b, a, num_in, den_in, b_last, m_loc, dc, dn))
    return from_chunks(h), c_f, n_f, m_f

def mlstm_project(h, w_in, gate_b):
    bsz, l, _ = h.shape
    nqk, nv = MLSTM_HEADS * MLSTM_DQK, MLSTM_HEADS * MLSTM_DV
    z = h @ w_in
    q = z[..., :nqk].reshape(bsz, l, MLSTM_HEADS, MLSTM_DQK).astype(F32) * (MLSTM_DQK ** -0.5)
    k = z[..., nqk:2 * nqk].reshape(bsz, l, MLSTM_HEADS, MLSTM_DQK).astype(F32)
    v = z[..., 2 * nqk:2 * nqk + nv].reshape(bsz, l, MLSTM_HEADS, MLSTM_DV).astype(F32)
    o_gate = z[..., 2 * nqk + nv:2 * nqk + 2 * nv]
    gates = z[..., 2 * nqk + 2 * nv:].reshape(bsz, l, 2, 2, MLSTM_HEADS).astype(F32) + gate_b.astype(F32)
    ig = gates[:, :, :, 0]
    lf = jax.nn.log_sigmoid(gates[:, :, :, 1])
    return q, k, v, ig, lf, o_gate

def mlstm_mixer(h_ctx, h_lat, want_ctx, w_in, gate_b, norm_g, w_out):
    qc, kc, vc, igc, lfc, og_c = mlstm_project(h_ctx, w_in, gate_b)
    ql, kl, vl, igl, lfl, og_l = mlstm_project(h_lat, w_in, gate_b)
    bsz = h_ctx.shape[0]
    c0 = jnp.zeros((bsz, MLSTM_HEADS, MLSTM_DQK, MLSTM_DV), F32)
    n0 = jnp.zeros((bsz, MLSTM_HEADS, MLSTM_DQK), F32)
    m0 = jnp.zeros((bsz, MLSTM_HEADS), F32)
    o_ctx, o_lat = [], []
    for d, f in enumerate((identity, flip_seq)):
        hc, cc, nc, mc = mlstm_chunked(f(qc), f(kc), f(vc), f(igc[:, :, d]), f(lfc[:, :, d]), c0, n0, m0)
        hl, _, _, _ = mlstm_chunked(f(ql), f(kl), f(vl), f(igl[:, :, d]), f(lfl[:, :, d]), cc, nc, mc)
        o_ctx.append(f(hc))
        o_lat.append(f(hl))

    def finish(h_pair, o_gate, dtype):
        o = rms_norm(h_pair[0] + h_pair[1], norm_g)
        o = o.reshape(*o.shape[:2], MLSTM_HEADS * MLSTM_DV) * jax.nn.sigmoid(o_gate.astype(F32))
        return o.astype(dtype) @ w_out

    y_ctx = finish(o_ctx, og_c, h_ctx.dtype) if want_ctx else None
    return y_ctx, finish(o_lat, og_l, h_lat.dtype)

def axial_rope(seq_len):
    rows = seq_len // GRID_W
    row = jnp.repeat(jnp.arange(rows), GRID_W).astype(F32)
    col = jnp.tile(jnp.arange(GRID_W), rows).astype(F32)
    n_pair = ATTN_DH // 4
    inv = ROPE_THETA ** (-jnp.arange(n_pair, dtype=F32) / n_pair)
    ang = jnp.concatenate([row[:, None] * inv, col[:, None] * inv], axis=-1)
    return jnp.cos(ang), jnp.sin(ang)

def apply_rope(x, cos, sin):
    xr = x.reshape(*x.shape[:-1], -1, 2)
    x0, x1 = xr[..., 0], xr[..., 1]
    cos = cos.astype(x.dtype)
    sin = sin.astype(x.dtype)
    return jnp.stack([x0 * cos - x1 * sin, x0 * sin + x1 * cos], axis=-1).reshape(x.shape)

def attend(q, k, v):
    s = jnp.einsum("bqhgd,bkhd->bhgqk", q, k, preferred_element_type=F32) * (ATTN_DH ** -0.5)
    p = jax.nn.softmax(s, axis=-1).astype(v.dtype)
    return jnp.einsum("bhgqk,bkhd->bqhgd", p, v)

def gqa_mixer(h_ctx, h_lat, want_ctx, w_in, q_norm_g, k_norm_g, w_out):
    nq, nk = ATTN_HEADS * ATTN_DH, ATTN_KV_HEADS * ATTN_DH

    def project(h):
        bsz, l, _ = h.shape
        z = h @ w_in
        q = rms_norm(z[..., :nq].reshape(bsz, l, ATTN_KV_HEADS, ATTN_GROUP, ATTN_DH), q_norm_g)
        k = rms_norm(z[..., nq:nq + nk].reshape(bsz, l, ATTN_KV_HEADS, ATTN_DH), k_norm_g)
        v = z[..., nq + nk:].reshape(bsz, l, ATTN_KV_HEADS, ATTN_DH)
        return q, k, v

    qc, kc, vc = project(h_ctx)
    ql, kl, vl = project(h_lat)
    bsz, l = h_lat.shape[:2]
    cos, sin = axial_rope(l)
    ql = apply_rope(ql, cos[:, None, None, :], sin[:, None, None, :])
    kl = apply_rope(kl, cos[:, None, :], sin[:, None, :])
    k_all = jnp.concatenate([kc, kl], axis=1)
    v_all = jnp.concatenate([vc, vl], axis=1)
    nb = l // Q_BLOCK
    qb = jnp.moveaxis(ql.reshape(bsz, nb, Q_BLOCK, ATTN_KV_HEADS, ATTN_GROUP, ATTN_DH), 1, 0)
    ob = lax.map(lambda qq: attend(qq, k_all, v_all), qb)
    y_lat = jnp.moveaxis(ob, 0, 1).reshape(bsz, l, nq) @ w_out
    y_ctx = attend(qc, kc, vc).reshape(bsz, h_ctx.shape[1], nq) @ w_out if want_ctx else None
    return y_ctx, y_lat

def conv_glu(h, w_in, conv_w, conv_b, w_out):
    val, gate = jnp.split(h @ w_in, 2, axis=-1)
    gate = dw_conv(gate, conv_w) + conv_b
    return (val * jax.nn.silu(gate)) @ w_out

def _count(kind):
    return len(range(kind, DEPTH, N_MIXERS))

def first_inputs(seed: int = 0) -> dict:
    key = jax.random.key(seed)
    keys = iter(jax.random.split(key, 40))

    def nrm(shape, std):
        return std * jax.random.normal(next(keys), shape, F32)

    D = D_MODEL
    n_a, n_b, n_c = _count(0), _count(1), _count(2)
    x = nrm((BATCH, SEQ, D), 1.0)
    c = nrm((BATCH, D), 1.0)
    ctx = nrm((BATCH, CTX_LEN, D), 1.0)
    c_ctx = nrm((D,), 1.0)
    norm1_g = 1.0 + nrm((DEPTH, D), 0.02)
    norm2_g = 1.0 + nrm((DEPTH, D), 0.02)
    w_mod = nrm((DEPTH, D, 6 * D), 0.5 * D ** -0.5)
    b_mod = nrm((DEPTH, 6 * D), 0.02)
    ffn_w_in = nrm((DEPTH, D, 2 * FFN_DIM), D ** -0.5)
    ffn_conv_w = nrm((DEPTH, FFN_CONV, FFN_DIM), FFN_CONV ** -0.5)
    ffn_conv_b = nrm((DEPTH, FFN_DIM), 0.02)
    ffn_w_out = nrm((DEPTH, FFN_DIM, D), FFN_DIM ** -0.5)
    gdn_w_in = nrm((n_a, D, GDN_IN), D ** -0.5)
    gdn_conv_w = nrm((n_a, GDN_CONV, 2 * GDN_HEADS * GDN_DK + GDN_HEADS * GDN_DV), GDN_CONV ** -0.5)
    gdn_a_log = jnp.log(jax.random.uniform(next(keys), (n_a, 2, GDN_HEADS), F32, 1.0, 16.0))
    dt = jnp.exp(jax.random.uniform(next(keys), (n_a, 2, GDN_HEADS), F32, math.log(1e-3), math.log(1e-1)))
    gdn_dt_bias = dt + jnp.log(-jnp.expm1(-dt))
    gdn_norm_g = 1.0 + nrm((n_a, GDN_DV), 0.02)
    gdn_w_out = nrm((n_a, GDN_HEADS * GDN_DV, D), (GDN_HEADS * GDN_DV) ** -0.5)
    mlstm_w_in = nrm((n_b, D, MLSTM_IN), D ** -0.5)
    ig_b = nrm((n_b, 2, 1, MLSTM_HEADS), 0.1)
    fg_b = jnp.linspace(3.0, 6.0, MLSTM_HEADS, dtype=F32) + nrm((n_b, 2, 1, MLSTM_HEADS), 0.1)
    mlstm_gate_b = jnp.concatenate([ig_b, fg_b], axis=2)
    mlstm_norm_g = 1.0 + nrm((n_b, MLSTM_DV), 0.02)
    mlstm_w_out = nrm((n_b, MLSTM_HEADS * MLSTM_DV, D), (MLSTM_HEADS * MLSTM_DV) ** -0.5)
    attn_w_in = nrm((n_c, D, ATTN_IN), D ** -0.5)
    attn_q_norm_g = 1.0 + nrm((n_c, ATTN_DH), 0.02)
    attn_k_norm_g = 1.0 + nrm((n_c, ATTN_DH), 0.02)
    attn_w_out = nrm((n_c, ATTN_HEADS * ATTN_DH, D), (ATTN_HEADS * ATTN_DH) ** -0.5)
    final_norm_g = 1.0 + nrm((D,), 0.02)
    return {
        "x": x, "c": c, "ctx": ctx, "c_ctx": c_ctx,
        "norm1_g": norm1_g, "norm2_g": norm2_g, "w_mod": w_mod, "b_mod": b_mod,
        "ffn_w_in": ffn_w_in, "ffn_conv_w": ffn_conv_w, "ffn_conv_b": ffn_conv_b, "ffn_w_out": ffn_w_out,
        "gdn_w_in": gdn_w_in, "gdn_conv_w": gdn_conv_w, "gdn_a_log": gdn_a_log, "gdn_dt_bias": gdn_dt_bias,
        "gdn_norm_g": gdn_norm_g, "gdn_w_out": gdn_w_out,
        "mlstm_w_in": mlstm_w_in, "mlstm_gate_b": mlstm_gate_b, "mlstm_norm_g": mlstm_norm_g,
        "mlstm_w_out": mlstm_w_out,
        "attn_w_in": attn_w_in, "attn_q_norm_g": attn_q_norm_g, "attn_k_norm_g": attn_k_norm_g,
        "attn_w_out": attn_w_out, "final_norm_g": final_norm_g,
    }

def first_block(x, c, ctx, c_ctx, norm1_g, norm2_g, w_mod, b_mod, ffn_w_in, ffn_conv_w, ffn_conv_b,
              ffn_w_out, gdn_w_in, gdn_conv_w, gdn_a_log, gdn_dt_bias, gdn_norm_g, gdn_w_out,
              mlstm_w_in, mlstm_gate_b, mlstm_norm_g, mlstm_w_out, attn_w_in, attn_q_norm_g,
              attn_k_norm_g, attn_w_out, final_norm_g):
    x_lat, x_ctx = x, ctx
    s_lat = jax.nn.silu(c)[:, None, :]
    s_ctx = jax.nn.silu(c_ctx)[None, None, :]
    for i in range(DEPTH):
        last = i == DEPTH - 1
        kind, j = i % N_MIXERS, i // N_MIXERS
        mod_l = jnp.split(s_lat @ w_mod[i] + b_mod[i], 6, axis=-1)
        mod_c = jnp.split(s_ctx @ w_mod[i] + b_mod[i], 6, axis=-1)
        h_lat = modulate(rms_norm(x_lat, norm1_g[i]), mod_l[0], mod_l[1])
        h_ctx = modulate(rms_norm(x_ctx, norm1_g[i]), mod_c[0], mod_c[1])
        if kind == 0:
            y_ctx, y_lat = gdn_mixer(h_ctx, h_lat, not last, gdn_w_in[j], gdn_conv_w[j], gdn_a_log[j],
                                     gdn_dt_bias[j], gdn_norm_g[j], gdn_w_out[j])
        elif kind == 1:
            y_ctx, y_lat = mlstm_mixer(h_ctx, h_lat, not last, mlstm_w_in[j], mlstm_gate_b[j],
                                       mlstm_norm_g[j], mlstm_w_out[j])
        else:
            y_ctx, y_lat = gqa_mixer(h_ctx, h_lat, not last, attn_w_in[j], attn_q_norm_g[j],
                                     attn_k_norm_g[j], attn_w_out[j])
        x_lat = x_lat + mod_l[2] * y_lat
        h_lat = modulate(rms_norm(x_lat, norm2_g[i]), mod_l[3], mod_l[4])
        x_lat = x_lat + mod_l[5] * conv_glu(h_lat, ffn_w_in[i], ffn_conv_w[i], ffn_conv_b[i], ffn_w_out[i])
        if not last:
            x_ctx = x_ctx + mod_c[2] * y_ctx
            h_ctx = modulate(rms_norm(x_ctx, norm2_g[i]), mod_c[3], mod_c[4])
            x_ctx = x_ctx + mod_c[5] * conv_glu(h_ctx, ffn_w_in[i], ffn_conv_w[i], ffn_conv_b[i], ffn_w_out[i])
    return rms_norm(x_lat, final_norm_g)


DEPTH_2 = 2

N_EVEN = (DEPTH_2 + 1) // 2
N_ODD = DEPTH_2 // 2
RMS_EPS = 1e-6

A_HEADS = 8
A_KV_HEADS = 2
A_HEAD_DIM = 64
A_WINDOW = 128
B_HEADS = 4
B_KEY_DIM = 64
B_VAL_DIM = 128
B_GATE_RANK = 16
B_GATE_TAU = 16.0
B_CHUNK = 64
C_HEADS = 8
C_HEAD_DIM = 128
C_BLOCK = 256
C_TOPK = 3
C_ROW_BLOCK = 128
REL_BUCKETS = 32
REL_MAX_DIST = 128
REL_HEADS = 8
MOE_GROUPS = 4
MOE_EXPERTS_PER_GROUP = 8
MOE_EXPERTS = MOE_GROUPS * MOE_EXPERTS_PER_GROUP
MOE_TOPK = 2
MOE_HIDDEN = 512
MOE_ROW_BLOCK = 128

EVEN_SPLITS = (A_HEADS * A_HEAD_DIM, A_KV_HEADS * A_HEAD_DIM, A_KV_HEADS * A_HEAD_DIM,
               B_HEADS * B_KEY_DIM, B_HEADS * B_KEY_DIM, B_HEADS * B_VAL_DIM,
               B_HEADS * B_VAL_DIM, B_GATE_RANK)
EVEN_IN = sum(EVEN_SPLITS)
EVEN_MIX = A_HEADS * A_HEAD_DIM + B_HEADS * B_VAL_DIM
ODD_MIX = C_HEADS * C_HEAD_DIM


def _rms(x, w):
    xf = x.astype(jnp.float32)
    y = xf * lax.rsqrt(jnp.mean(xf * xf, axis=-1, keepdims=True) + RMS_EPS)
    return (y * w.astype(jnp.float32)).astype(x.dtype)

def _rel_bucket(dist):
    exact = REL_BUCKETS // 2
    d = jnp.maximum(dist, 0)
    logd = jnp.log(jnp.maximum(d, 1).astype(jnp.float32) / exact) / math.log(REL_MAX_DIST / exact)
    far = jnp.minimum(exact + (logd * (REL_BUCKETS - exact)).astype(jnp.int32), REL_BUCKETS - 1)
    return jnp.where(d < exact, d, far)

def _group_rows(ids, n_groups, rows):
    n = ids.shape[0]
    n_rows = ((n + rows - 1) // rows) * rows + n_groups * rows
    counts = jnp.zeros((n_groups + 1,), jnp.int32).at[ids].add(1)[:n_groups]
    padded = ((counts + rows - 1) // rows) * rows
    start = jnp.cumsum(counts) - counts
    pend = jnp.cumsum(padded)
    pstart = pend - padded
    order = jnp.argsort(ids)
    sid = ids[order]
    gid = jnp.minimum(sid, n_groups - 1)
    dest = jnp.where(sid < n_groups, pstart[gid] + jnp.arange(n) - start[gid], n_rows)
    src = jnp.full((n_rows,), n, jnp.int32).at[dest].set(order.astype(jnp.int32), mode='drop')
    blk_group = jnp.searchsorted(pend, jnp.arange(n_rows // rows) * rows, side='right')
    return src, jnp.minimum(blk_group, n_groups - 1)

def _swa_sink_attention(q, k, v, sinks, rel_bias):
    B, S, _, hd = q.shape
    W = A_WINDOW
    nb = S // W
    G = A_HEADS // A_KV_HEADS
    f32 = jnp.float32
    qb = q.reshape(B, nb, W, A_KV_HEADS, G, hd)

    def band(t):
        tb = t.reshape(B, nb, W, A_KV_HEADS, hd)
        prev = jnp.pad(tb, ((0, 0), (1, 0), (0, 0), (0, 0), (0, 0)))[:, :-1]
        return jnp.concatenate([prev, tb], axis=2)

    kband, vband = band(k), band(v)
    lg = jnp.einsum('bnqkgd,bnskd->bkgnqs', qb, kband, preferred_element_type=f32) * hd ** -0.5
    dist = jnp.arange(W)[:, None] + W - jnp.arange(2 * W)[None, :]
    mask = ((dist >= 0) & (dist < W)
            & ((jnp.arange(nb)[:, None, None] > 0) | (jnp.arange(2 * W) >= W)[None, None, :]))
    bias = rel_bias[_rel_bucket(dist)].transpose(2, 0, 1).reshape(A_KV_HEADS, G, 1, W, 2 * W)
    lg = jnp.where(mask, lg + bias, -jnp.inf)
    sink = sinks.astype(f32).reshape(A_KV_HEADS, G, 1, 1, 1)
    m = jnp.maximum(lg.max(-1, keepdims=True), sink)
    p = jnp.exp(lg - m)
    probs = p / (p.sum(-1, keepdims=True) + jnp.exp(sink - m))
    o = jnp.einsum('bkgnqs,bnskd->bnqkgd', probs.astype(v.dtype), vband, preferred_element_type=f32)
    return o.reshape(B, S, A_HEADS * hd)

def _gla(q, k, v, log_a):
    B, S, H, dk = q.shape
    dv = v.shape[-1]
    C = B_CHUNK
    n = S // C

    def chunks(t):
        return t.reshape(B, n, C, H, t.shape[-1]).transpose(0, 3, 1, 2, 4)

    q, k, v, g = chunks(q * dk ** -0.5), chunks(k), chunks(v), chunks(log_a)
    b = jnp.cumsum(g, axis=3)
    b_last = b[:, :, :, -1:]
    q_dec = q * jnp.exp(b)
    att = jnp.einsum('bhnid,bhnjd->bhnij', q_dec, k * jnp.exp(-b))
    att = jnp.where(jnp.tril(jnp.ones((C, C), bool)), att, 0.0)
    o_intra = jnp.einsum('bhnij,bhnjv->bhniv', att, v)
    upd = jnp.einsum('bhnjd,bhnjv->bhndv', k * jnp.exp(b_last - b), v)
    decay = jnp.exp(b_last[:, :, :, 0])

    def step(state, inp):
        dec, u = inp
        return state * dec[..., None] + u, state

    _, s_in = lax.scan(step, jnp.zeros((B, H, dk, dv), q.dtype),
                       (decay.transpose(2, 0, 1, 3), upd.transpose(2, 0, 1, 3, 4)))
    o_inter = jnp.einsum('bhnid,bhndv->bhniv', q_dec, s_in.transpose(1, 2, 0, 3, 4))
    return (o_intra + o_inter).transpose(0, 2, 3, 1, 4).reshape(B, S, H, dv)

def _moba(q, k, v, rel_bias):
    B, S, H, hd = q.shape
    L = C_BLOCK
    nb = -(-S // L)
    Sp = nb * L
    k_sel = min(C_TOPK, nb)
    scale = hd ** -0.5
    f32 = jnp.float32
    q, k, v = [jnp.pad(t, ((0, 0), (0, Sp - S), (0, 0), (0, 0))).transpose(0, 2, 1, 3) for t in (q, k, v)]
    qb = q.reshape(B, H, nb, L, hd)
    kb = k.reshape(B, H, nb, L, hd)
    vb = v.reshape(B, H, nb, L, hd)
    li = jnp.arange(L)
    d_own = li[:, None] - li[None, :]
    bias_own = rel_bias[_rel_bucket(d_own)].transpose(2, 0, 1)[None, :, None]
    lg = jnp.einsum('bhnqd,bhnsd->bhnqs', qb, kb, preferred_element_type=f32) * scale + bias_own
    lg = jnp.where(d_own >= 0, lg, -jnp.inf)
    lse_own = jax.nn.logsumexp(lg, axis=-1)
    o_own = jnp.einsum('bhnqs,bhnsd->bhnqd', jnp.exp(lg - lse_own[..., None]).astype(v.dtype), vb,
                       preferred_element_type=f32)
    pos = jnp.arange(Sp)
    qblk = pos // L
    score = jnp.einsum('bhtd,bhjd->bhtj', q.astype(f32), kb.astype(f32).mean(axis=3))
    score = jnp.where(jnp.arange(nb)[None, :] < qblk[:, None], score, -jnp.inf)
    _, sel = lax.top_k(score, k_sel)
    valid = (jnp.arange(k_sel)[None, :] < jnp.minimum(qblk, k_sel)[:, None]) & (pos < S)[:, None]
    n_groups = B * H * nb
    grp = jnp.arange(B * H).reshape(B, H, 1, 1) * nb + sel
    grp = jnp.where(valid, grp, n_groups).reshape(-1)
    src, blk_grp = _group_rows(grp, n_groups, C_ROW_BLOCK)
    n_pairs = grp.shape[0]
    row_ok = src < n_pairs
    row_tok = jnp.minimum(src, n_pairs - 1) // k_sel
    n_tok = B * H * Sp
    q_rows = q.reshape(n_tok, hd)
    k_grp = kb.reshape(n_groups, L, hd)
    v_grp = vb.reshape(n_groups, L, hd)

    def attend_block(args):
        tok, g = args
        qr = q_rows[tok]
        dist = (tok % Sp)[:, None] - ((g % nb) * L + li)[None, :]
        bias = rel_bias[_rel_bucket(dist), (g // nb) % H]
        lg_r = jnp.einsum('rd,sd->rs', qr, k_grp[g], preferred_element_type=f32) * scale + bias
        lse_r = jax.nn.logsumexp(lg_r, axis=-1)
        o_r = jnp.einsum('rs,sd->rd', jnp.exp(lg_r - lse_r[:, None]).astype(v.dtype), v_grp[g],
                         preferred_element_type=f32)
        return o_r, lse_r

    o_sel, lse_sel = lax.map(attend_block, (row_tok.reshape(-1, C_ROW_BLOCK), blk_grp))
    o_sel = o_sel.reshape(-1, hd)
    lse_sel = lse_sel.reshape(-1)
    seg = jnp.where(row_ok, row_tok, n_tok)
    lse_own = lse_own.reshape(n_tok)
    m_sel = jax.ops.segment_max(jnp.where(row_ok, lse_sel, -jnp.inf), seg, num_segments=n_tok + 1)[:n_tok]
    m = jnp.maximum(lse_own, m_sel)
    w_sel = jnp.where(row_ok, jnp.exp(lse_sel - m[jnp.minimum(seg, n_tok - 1)]), 0.0)
    w_own = jnp.exp(lse_own - m)
    num = (w_own[:, None] * o_own.reshape(n_tok, hd)
           + jax.ops.segment_sum(w_sel[:, None] * o_sel, seg, num_segments=n_tok + 1)[:n_tok])
    den = w_own + jax.ops.segment_sum(w_sel, seg, num_segments=n_tok + 1)[:n_tok]
    o = (num / den[:, None]).reshape(B, H, Sp, hd)[:, :, :S]
    return o.transpose(0, 2, 1, 3).reshape(B, S, H * hd).astype(q.dtype)

def _even_mixer(h, w_in, w_out, q_norm, k_norm, sinks, gate_up, gate_bias, out_norm, rel_bias):
    B, S, _ = h.shape
    f32 = jnp.float32
    qa, ka, va, qb, kb, vb, rb, ab = jnp.split(h @ w_in, np.cumsum(EVEN_SPLITS)[:-1].tolist(), axis=-1)
    qa = _rms(qa.reshape(B, S, A_HEADS, A_HEAD_DIM), q_norm)
    ka = _rms(ka.reshape(B, S, A_KV_HEADS, A_HEAD_DIM), k_norm)
    va = va.reshape(B, S, A_KV_HEADS, A_HEAD_DIM)
    oa = _swa_sink_attention(qa, ka, va, sinks, rel_bias).astype(h.dtype)
    log_a = jax.nn.log_sigmoid((ab @ gate_up + gate_bias).astype(f32)) / B_GATE_TAU
    ob = _gla(qb.reshape(B, S, B_HEADS, B_KEY_DIM).astype(f32),
              kb.reshape(B, S, B_HEADS, B_KEY_DIM).astype(f32),
              vb.reshape(B, S, B_HEADS, B_VAL_DIM).astype(f32),
              log_a.reshape(B, S, B_HEADS, B_KEY_DIM))
    ob = _rms(ob, out_norm).astype(h.dtype) * jax.nn.silu(rb).reshape(B, S, B_HEADS, B_VAL_DIM)
    return jnp.concatenate([oa, ob.reshape(B, S, B_HEADS * B_VAL_DIM)], axis=-1) @ w_out

def _odd_mixer(h, w_in, w_out, q_norm, k_norm, rel_bias):
    B, S, _ = h.shape
    q, k, v = jnp.split(h @ w_in, 3, axis=-1)
    q = _rms(q.reshape(B, S, C_HEADS, C_HEAD_DIM), q_norm)
    k = _rms(k.reshape(B, S, C_HEADS, C_HEAD_DIM), k_norm)
    v = v.reshape(B, S, C_HEADS, C_HEAD_DIM)
    return _moba(q, k, v, rel_bias) @ w_out

def _hier_moe(h, w_group, b_group, w_expert, b_expert, w1, w3, w2):
    B, S, D = h.shape
    N = B * S
    f32 = jnp.float32
    xt = h.reshape(N, D)
    g_logits = (xt @ w_group).astype(f32) + b_group.astype(f32)
    g_sel = jnp.argmax(g_logits, axis=-1)
    p_g = jnp.take_along_axis(jax.nn.softmax(g_logits, axis=-1), g_sel[:, None], axis=-1)
    e_logits = ((xt @ w_expert).astype(f32) + b_expert.astype(f32)).reshape(N, MOE_GROUPS, MOE_EXPERTS_PER_GROUP)
    e_in = jnp.take_along_axis(e_logits, g_sel[:, None, None], axis=1)[:, 0]
    top_v, top_i = lax.top_k(e_in, MOE_TOPK)
    gate = (p_g * jax.nn.softmax(top_v, axis=-1)).reshape(-1)
    ids = (g_sel[:, None] * MOE_EXPERTS_PER_GROUP + top_i).reshape(-1)
    src, blk_e = _group_rows(ids, MOE_EXPERTS, MOE_ROW_BLOCK)
    n_pairs = ids.shape[0]
    row_ok = src < n_pairs
    pair = jnp.minimum(src, n_pairs - 1)
    row_tok = pair // MOE_TOPK

    def expert_block(args):
        tok, e = args
        xr = xt[tok]
        return (jax.nn.silu(xr @ w1[e]) * (xr @ w3[e])) @ w2[e]

    y = lax.map(expert_block, (row_tok.reshape(-1, MOE_ROW_BLOCK), blk_e)).reshape(-1, D)
    w_row = jnp.where(row_ok, gate[pair], 0.0).astype(y.dtype)
    seg = jnp.where(row_ok, row_tok, N)
    out = jax.ops.segment_sum(y * w_row[:, None], seg, num_segments=N + 1)[:N]
    return out.reshape(B, S, D)

def second_inputs(seed: int = 0) -> dict:
    key = jax.random.key(seed)
    ks = iter(jax.random.split(key, 32))
    D = D_MODEL

    def nrm(shape, s):
        return jax.random.normal(next(ks), shape, jnp.float32) * s

    return {
        'x': nrm((BATCH, SEQ, D), 1.0),
        'c': nrm((BATCH, D), 1.0),
        'rel_bias': nrm((REL_BUCKETS, REL_HEADS), 0.5),
        'ada_w': nrm((DEPTH_2, D, 6 * D), 0.5 * D ** -0.5),
        'ada_b': nrm((DEPTH_2, 6 * D), 0.02),
        'norm1_w': 1.0 + nrm((DEPTH_2, D), 0.05),
        'norm2_w': 1.0 + nrm((DEPTH_2, D), 0.05),
        'even_w_in': nrm((N_EVEN, D, EVEN_IN), D ** -0.5),
        'even_w_out': nrm((N_EVEN, EVEN_MIX, D), EVEN_MIX ** -0.5),
        'a_q_norm': 1.0 + nrm((N_EVEN, A_HEAD_DIM), 0.05),
        'a_k_norm': 1.0 + nrm((N_EVEN, A_HEAD_DIM), 0.05),
        'a_sinks': nrm((N_EVEN, A_HEADS), 0.5),
        'b_gate_up': nrm((N_EVEN, B_GATE_RANK, B_HEADS * B_KEY_DIM), B_GATE_RANK ** -0.5),
        'b_gate_bias': nrm((N_EVEN, B_HEADS * B_KEY_DIM), 0.1),
        'b_out_norm': 1.0 + nrm((N_EVEN, B_VAL_DIM), 0.05),
        'odd_w_in': nrm((N_ODD, D, 3 * ODD_MIX), D ** -0.5),
        'odd_w_out': nrm((N_ODD, ODD_MIX, D), ODD_MIX ** -0.5),
        'c_q_norm': 1.0 + nrm((N_ODD, C_HEAD_DIM), 0.05),
        'c_k_norm': 1.0 + nrm((N_ODD, C_HEAD_DIM), 0.05),
        'moe_w_group': nrm((DEPTH_2, D, MOE_GROUPS), D ** -0.5),
        'moe_b_group': nrm((DEPTH_2, MOE_GROUPS), 0.01),
        'moe_w_expert': nrm((DEPTH_2, D, MOE_EXPERTS), D ** -0.5),
        'moe_b_expert': nrm((DEPTH_2, MOE_EXPERTS), 0.01),
        'moe_w1': nrm((DEPTH_2, MOE_EXPERTS, D, MOE_HIDDEN), D ** -0.5),
        'moe_w3': nrm((DEPTH_2, MOE_EXPERTS, D, MOE_HIDDEN), D ** -0.5),
        'moe_w2': nrm((DEPTH_2, MOE_EXPERTS, MOE_HIDDEN, D), MOE_HIDDEN ** -0.5),
    }

def second_block(x, c, rel_bias, ada_w, ada_b, norm1_w, norm2_w, even_w_in, even_w_out, a_q_norm,
              a_k_norm, a_sinks, b_gate_up, b_gate_bias, b_out_norm, odd_w_in, odd_w_out, c_q_norm,
              c_k_norm, moe_w_group, moe_b_group, moe_w_expert, moe_b_expert, moe_w1, moe_w3, moe_w2):
    cond = jax.nn.silu(c)
    for layer in range(DEPTH_2):
        mod = (cond @ ada_w[layer] + ada_b[layer])[:, None, :]
        shift1, scale1, gate1, shift2, scale2, gate2 = jnp.split(mod, 6, axis=-1)
        h = _rms(x, norm1_w[layer]) * (1 + scale1) + shift1
        j = layer // 2
        if layer % 2 == 0:
            y = _even_mixer(h, even_w_in[j], even_w_out[j], a_q_norm[j], a_k_norm[j], a_sinks[j],
                            b_gate_up[j], b_gate_bias[j], b_out_norm[j], rel_bias)
        else:
            y = _odd_mixer(h, odd_w_in[j], odd_w_out[j], c_q_norm[j], c_k_norm[j], rel_bias)
        x = x + gate1 * y
        h = _rms(x, norm2_w[layer]) * (1 + scale2) + shift2
        x = x + gate2 * _hier_moe(h, moe_w_group[layer], moe_b_group[layer], moe_w_expert[layer],
                                  moe_b_expert[layer], moe_w1[layer], moe_w3[layer], moe_w2[layer])
    return x


def setup_inputs(seed=0):
    out = dict(first_inputs(seed))
    for name, value in second_inputs(seed + 1).items():
        if name != "x":
            out[name + "_2"] = value
    return out


def reference(
    x, c, ctx, c_ctx, norm1_g, norm2_g, w_mod, b_mod, ffn_w_in, ffn_conv_w, ffn_conv_b,
    ffn_w_out, gdn_w_in, gdn_conv_w, gdn_a_log, gdn_dt_bias, gdn_norm_g, gdn_w_out, mlstm_w_in,
    mlstm_gate_b, mlstm_norm_g, mlstm_w_out, attn_w_in, attn_q_norm_g, attn_k_norm_g,
    attn_w_out, final_norm_g, c_2, rel_bias_2, ada_w_2, ada_b_2, norm1_w_2, norm2_w_2,
    even_w_in_2, even_w_out_2, a_q_norm_2, a_k_norm_2, a_sinks_2, b_gate_up_2, b_gate_bias_2,
    b_out_norm_2, odd_w_in_2, odd_w_out_2, c_q_norm_2, c_k_norm_2, moe_w_group_2, moe_b_group_2,
    moe_w_expert_2, moe_b_expert_2, moe_w1_2, moe_w3_2, moe_w2_2,
):
    x = first_block(
        x, c, ctx, c_ctx, norm1_g, norm2_g, w_mod, b_mod, ffn_w_in, ffn_conv_w, ffn_conv_b,
        ffn_w_out, gdn_w_in, gdn_conv_w, gdn_a_log, gdn_dt_bias, gdn_norm_g, gdn_w_out,
        mlstm_w_in, mlstm_gate_b, mlstm_norm_g, mlstm_w_out, attn_w_in, attn_q_norm_g,
        attn_k_norm_g, attn_w_out, final_norm_g,
    )
    return second_block(
        x, c_2, rel_bias_2, ada_w_2, ada_b_2, norm1_w_2, norm2_w_2, even_w_in_2, even_w_out_2,
        a_q_norm_2, a_k_norm_2, a_sinks_2, b_gate_up_2, b_gate_bias_2, b_out_norm_2, odd_w_in_2,
        odd_w_out_2, c_q_norm_2, c_k_norm_2, moe_w_group_2, moe_b_group_2, moe_w_expert_2,
        moe_b_expert_2, moe_w1_2, moe_w3_2, moe_w2_2,
    )


_drawn_inputs = setup_inputs


def setup_inputs(seed=0):
    import zlib

    import numpy as np

    out = dict(_drawn_inputs(seed))
    spreads = {}
    factors = {'ctx': 3.246,
     'c_ctx': 4.766,
     'norm1_g': 6.202,
     'norm2_g': 5.191,
     'ffn_conv_b': 7.248,
     'gdn_norm_g': 8.0,
     'norm1_w_2': 2.846,
     'a_q_norm_2': 8.0,
     'a_k_norm_2': 8.0,
     'a_sinks_2': 31.256,
     'b_gate_bias_2': 4.977,
     'b_out_norm_2': 4.889,
     'c_q_norm_2': 8.0,
     'c_k_norm_2': 8.0,
     'moe_b_group_2': 6.79,
     'moe_b_expert_2': 8.0}
    for name, (base, spread) in spreads.items():
        noise = np.random.default_rng([zlib.crc32(name.encode()), seed]).standard_normal(out[name].shape)
        drawn = base * np.exp(spread * noise) if base else spread * noise
        out[name] = jnp.asarray(drawn.astype(out[name].dtype))
    for name, factor in factors.items():
        out[name] = (out[name] * factor).astype(out[name].dtype)
    return out
```

```python
import math

import numpy as np

import concourse.bass as bass
import concourse.mybir as mybir

F32 = mybir.dt.float32
I32 = mybir.dt.int32
U32 = mybir.dt.uint32
ALU = mybir.AluOpType
ACT = mybir.ActivationFunctionType
AX = mybir.AxisListType

P = 128
D = 1024
KD = D // P
L = 512
LB = L // P
LC = 256
H = 8
EPS = 1e-6
FFN = 2816
KF = FFN // P
NE, EH = 32, 512
NG, EG = 4, 8
OVF = 7
BLOCKS = NE + OVF
SLOTS = BLOCKS * P
NEG = -30000.0
RING = 6
BAND_LEN = 384

DENSE = [("mod1", 16), ("gdn_in", 32), ("mod2", 128), ("gdn_out", 8), ("ffn_in", 44), ("ffn_out", 22),
         ("even_in", 18), ("even_out", 8), ("odd_in", 24), ("odd_out", 8)]
TILE0, _n = {}, 0
for _name, _count in DENSE:
    TILE0[_name] = _n
    _n += _count
NTILES = _n

CONSTS = [("ident", 128), ("ones", 128), ("ones64", 128), ("tri_f", 128), ("tri_b", 128), ("neg_f", 128),
          ("neg_b", 128), ("pair_f", 128), ("pair_b", 128),
          ("levels", 6 * P), ("tri64", 128), ("stri", 128),
          ("swa", 256), ("causal", 256), ("iota_e", 32), ("iota_g", 4), ("grp", 32), ("slot0", 32),
          ("blk", 8), ("iota", 128), ("tok", 4), ("eps", 1), ("ln_dk", 1), ("bucket", BAND_LEN), ("flip", P)]
COL, _n = {}, 0
for _name, _count in CONSTS:
    COL[_name] = (_n, _count)
    _n += _count
NCONST = _n

SMALLS = [("c1", 16), ("mod_b", 144), ("norm1_g", 8), ("norm2_g", 8), ("final_g", 8), ("conv5", 24 * 5),
          ("gdn_norm", 1), ("a_log", 16), ("dt", 16), ("fconv", 22 * 3), ("fconv_b", 22), ("c2", 8),
          ("norm1_2", 16), ("norm2_2", 16), ("a_q", 1), ("a_k", 1), ("sinks", 8),
          ("b_norm", 1), ("c_q", 1), ("c_k", 1), ("moe_b", 72), ("rel", 8), ("gate_up", 256)]
SCOL, _n = {}, 0
for _name, _count in SMALLS:
    SCOL[_name] = (_n, _count)
    _n += _count
NSMALL = _n


def bucket_of(dist):
    exact = 16
    d = np.maximum(dist, 0)
    logd = np.log(np.maximum(d, 1).astype(np.float32) / np.float32(exact)) / np.float32(math.log(128 / exact))
    far = np.minimum(exact + (logd * np.float32(32 - exact)).astype(np.int32), 31)
    return np.where(d < exact, d, far)


def constant_tables():
    i = np.arange(P)
    row, col = i[:, None], i[None, :]
    t = {"ident": row == col, "ones": np.ones((P, P)), "ones64": row // 64 == col // 64,
         "tri_f": row <= col, "tri_b": row >= col,
         "neg_f": np.where(row <= col, 0.0, NEG), "neg_b": np.where(row >= col, 0.0, NEG),
         "tri64": (row <= col) & (row // 64 == col // 64), "stri": row < col}
    def between(level):
        b = 1 << level
        return -((row // (2 * b) == col // (2 * b)) & (row // b % 2 == 1) & (col // b % 2 == 0)).astype(float)

    t["pair_f"], t["pair_b"] = between(0).T, between(0)
    t["levels"] = np.concatenate([-(row // (1 << v) == col // (1 << v)).astype(float) for v in range(1, 7)], 1)
    dist = row + P - np.arange(2 * P)[None, :]
    t["swa"] = np.where((dist >= 0) & (dist < P), 0.0, NEG)
    t["causal"] = np.where(dist >= 0, 0.0, NEG)
    t["iota_e"] = np.tile(np.arange(32), (P, 1))
    t["iota_g"] = np.tile(np.arange(4), (P, 1))
    t["grp"] = np.tile(np.arange(32) // EG, (P, 1))
    t["slot0"] = np.tile(np.arange(32) * P, (P, 1))
    t["blk"] = np.tile(np.arange(8), (P, 1))
    t["iota"] = np.tile(i, (P, 1))
    t["tok"] = row + P * np.arange(4)[None, :]
    t["eps"] = np.full((P, 1), EPS)
    t["ln_dk"] = np.full((P, 1), -0.5 * math.log(P))
    t["flip"] = row + col == P - 1
    t["bucket"] = np.zeros((P, BAND_LEN))
    t["bucket"][bucket_of(255 - np.arange(BAND_LEN)), np.arange(BAND_LEN)] = 1
    return np.concatenate([np.asarray(t[n], np.float32) for n, _ in CONSTS], 1)


class Engine:

    def __init__(self, nc, name):
        self.sem, self.n = nc.alloc_semaphore(f"{name}_own_step"), 0

    def after(self, eng, ins):
        self.n += 1
        ins.then_inc(self.sem, 1)
        eng.wait_ge(self.sem, self.n)


class Program:
    def __init__(self, nc, ins, out):
        self.nc, self.ins, self.out = nc, ins, out
        self.sems, self.software_sems = {}, {}
        self.act, self.dve, self.pool = Engine(nc, "act"), Engine(nc, "dve"), Engine(nc, "pool")
        self.loaded = 0
        self.w_loaded = [nc.alloc_semaphore(f"w_loaded{i}") for i in range(RING)]
        self.w_done = nc.alloc_semaphore("w_done")
        self.output_stored = nc.alloc_semaphore("output_stored")
        total = 0

        def take(cols):
            nonlocal total
            total += cols
            return total - cols

        c0, s0, m0, x0, r0 = take(NCONST), take(NSMALL), take(8 * 48), take(KD * L), take(RING * D)
        self.free0 = total
        self.total = 53184
        self.arena = nc.alloc_sbuf_tensor("arena", [P, self.total], F32)
        self.bank = [nc.alloc_psum_tensor(f"bank{i}", [P, 512], F32) for i in range(8)]
        self.const_all, self.small_all = self.cols(c0, NCONST), self.cols(s0, NSMALL)
        self.c0, self.s0 = c0, s0
        self.mod_all = self.cols(m0, 144)
        self.mod = {n: self.cols(m0 + 48 * i, 48) for i, n in enumerate(
            ["lat", "even", "odd", "ctx", "g1", "g1c", "tmp", "tmp2"])}
        self.x = self.view(x0, KD, L)
        self.ring = self.view(r0, RING, D)
        self.rows = nc.dram_tensor("token_rows", [L, D], F32, kind="Internal")
        self.yrows = nc.dram_tensor("slot_rows", [SLOTS, D], F32, kind="Internal")
        self.gate_dram = nc.dram_tensor("gdn_gate", [P, H * L], F32, kind="Internal")
        self.band_dram = nc.dram_tensor("band_bias", [H, BAND_LEN], F32, kind="Internal")

    def cols(self, off, n):
        assert off + n <= self.total
        return self.arena[:, off:off + n]

    def view(self, off, a, b):
        assert off + a * b <= self.total, (off, a, b)
        return self.arena[:, off:off + a * b].rearrange("p (a b) -> p a b", a=a)

    def C(self, name):
        off, n = COL[name]
        return self.cols(self.c0 + off, n)

    def S(self, name, a=0, b=None):
        off, n = SCOL[name]
        return self.cols(self.s0 + off + a, (n if b is None else b) - a)

    def sem(self, name):
        if name not in self.sems:
            self.sems[name] = self.nc.alloc_semaphore(name)
        return self.sems[name]

    def software_sem(self, name):
        if name not in self.software_sems:
            self.software_sems[name] = self.nc.alloc_semaphore(name)
        return self.software_sems[name]

    def retire(self):
        with self.nc.Block() as block:
            @block.sync
            def _(sp):
                for sem in self.sems.values():
                    sp.sem_clear(sem)
        for sem in self.sems.values():
            self.nc.release_semaphore(sem)
        self.sems, self.residuals = {}, 0

    def load_until(self, eng, end):
        while self.loaded < min(end + RING, NTILES):
            n = self.loaded
            if n >= RING:
                eng.wait_ge(self.w_done, n - RING + 1)
            eng.dma_start(self.ring[:, n % RING, :], self.ins["dense"][n]).then_inc(self.w_loaded[n % RING], 16)
            self.loaded += 1

    def tile(self, eng, n):
        eng.wait_ge(self.w_loaded[n % RING], 16 * (n // RING + 1))
        return self.ring[:, n % RING, :].rearrange("p (k m) -> p k m", k=KD)

    def project(self, eng, w, dst, src):
        for k in range(KD):
            mm = eng.matmul(dst, w[:, k, :], src[:, k, :], start=(k == 0), stop=(k == KD - 1))
        return mm

    def load_inputs(self):
        nc, loaded = self.nc, self.sem("params_loaded")
        with nc.Block() as block:
            @block.sync
            def _(sp):
                sp.dma_start(self.const_all, self.ins["consts"][:, :]).then_inc(loaded, 16)
                sp.dma_start(self.small_all, self.ins["smalls"][:, :]).then_inc(loaded, 16)
                sp.dma_start(self.x, self.ins["xT"].rearrange("p (k t) -> p k t", k=KD)).then_inc(loaded, 16)
                self.load_until(sp, TILE0["mod1"])
                sp.wait_ge(loaded, 48)

    def modulations_1(self):
        nc = self.nc
        cs = self.view(self.free0, KD, 2)
        c1 = self.S("c1").rearrange("p (k s) -> p k s", k=KD)
        silu_done = self.sem("c1_silu")
        w0 = TILE0["mod1"]
        with nc.Block() as block:
            @block.sync
            def _(sp):
                self.load_until(sp, w0 + 16)

            @block.scalar
            def _(act):
                act.activation(cs, c1, ACT.Silu).then_inc(silu_done, 1)

            @block.vector
            def _(dve):
                dve.wait_ge(self.w_done, w0 + 16)
                mods = self.bank[0][:, 0:32].rearrange("p (m s) -> p m s", s=2)
                for s, name in enumerate(["lat", "ctx"]):
                    dve.tensor_tensor(self.mod[name][:, 0:16], mods[:, :, s], self.S("mod_b", 0, 16), ALU.add)

            @block.tensor
            def _(pe):
                pe.wait_ge(silu_done, 1)
                for m in range(16):
                    w = self.tile(pe, w0 + m)
                    self.project(pe, w, self.bank[0][:, 2 * m:2 * m + 2], cs).then_inc(self.w_done, 1)

    def norm(self, name, jobs, final=None):
        nc = self.nc
        sq, ss = self.sem(name + "_squares"), self.sem(name + "_sums")
        rs, nd = self.sem(name + "_rstd"), self.sem(name + "_scaled")
        r = [self.cols(self.total - 512 * (j + 1), 512) for j in range(len(jobs))]
        g1 = [self.mod["g1"], self.mod["g1c"]]
        with nc.Block() as block:
            @block.scalar
            def _(act):
                for j, (dst, src, n, *_) in enumerate(jobs):
                    for k in range(KD):
                        act.activation(dst[:, k, :], src[:, k, :], ACT.Square).then_inc(sq, 1)
                for j, (dst, src, n, gain, scale, shift) in enumerate(jobs):
                    act.wait_ge(ss, j + 1)
                    self.act.after(act, act.activation(r[j][:, 0:n], self.bank[j][:, 0:n], ACT.Ln,
                                                       scale=1.0 / D, bias=self.C("eps")))
                    act.activation(r[j][:, 0:n], r[j][:, 0:n], ACT.Exp, scale=-0.5).then_inc(rs, 1)
                for j, (dst, src, n, gain, scale, shift) in enumerate(jobs):
                    for k in range(KD):
                        act.wait_ge(nd, len(jobs) + KD * j + k + 1)
                        if shift is not None:
                            act.activation(dst[:, k, :], dst[:, k, :], ACT.Identity,
                                           scale=g1[j][:, k:k + 1], bias=shift[:, k:k + 1])
                        else:
                            act.activation(final[:, k, :], dst[:, k, :], ACT.Copy, scale=g1[j][:, k:k + 1])

            @block.tensor
            def _(pe):
                for j, (dst, src, n, *_) in enumerate(jobs):
                    for k in range(KD):
                        pe.wait_ge(sq, KD * j + k + 1)
                        mm = pe.matmul(self.bank[j][:, 0:n], self.C("ones"), dst[:, k, :],
                                       start=(k == 0), stop=(k == KD - 1))
                    mm.then_inc(ss, 1)

            @block.vector
            def _(dve):
                for j, (dst, src, n, gain, scale, shift) in enumerate(jobs):
                    g = g1[j][:, 0:KD]
                    if scale is not None:
                        self.dve.after(dve, dve.tensor_scalar(g, scale, 1.0, None, ALU.add))
                        dve.tensor_tensor(g, g, gain, ALU.mult).then_inc(nd, 1)
                    else:
                        dve.tensor_copy(g, gain).then_inc(nd, 1)
                for j, (dst, src, n, gain, scale, shift) in enumerate(jobs):
                    dve.wait_ge(rs, j + 1)
                    for k in range(KD):
                        dve.tensor_tensor(dst[:, k, :], src[:, k, :], r[j][:, 0:n], ALU.mult).then_inc(nd, 1)

    def gdn_layout(self):
        f = self.free0
        self.h = self.view(f, KD, L)
        self.hc = self.view(f + KD * L, KD, LC)
        self.vnat = self.view(f, 6, H * P)
        f += KD * (L + LC)
        self.qT = self.view(f, H, L)
        f += H * L
        self.kT = self.view(f, H, L + LC)
        f += H * (L + LC)
        self.vT = self.view(f, H, L + LC)
        self.knat = self.view(f, 6, H * P)
        f += H * (L + LC)
        self.g_free = f

    def gdn_project(self):
        nc = self.nc
        f = self.g_free
        gbuf = [self.cols(f + 1536 + 512 * i, 512) for i in range(2)]
        wba = self.view(f + 2560, KD, 32)
        self.ba = self.view(f + 2560 + 256, 6, 32)
        w0 = TILE0["gdn_in"]
        wba_in, centre, taps = self.sem("wba_loaded"), self.sem("conv_centre"), self.sem("conv_taps")
        silu_done = self.sem("gdn_silu")
        gate_out, ba_done = [self.software_sem(f"gate_stored{i}") for i in range(2)], self.sem("ba_projected")
        conv = self.S("conv5").rearrange("p (m j) -> p m j", m=24)

        def parts(m):
            b, c = self.bank[m % 3][:, :], self.bank[3 + m % 3][:, 0:LC]
            if m < 8:
                return [(self.qT[:, m, :], b)]
            if m < 24:
                dst = self.kT[:, m - 8, :] if m < 16 else self.vT[:, m - 16, :]
                return [(dst[:, 0:LC], c), (dst[:, LC:], b)]
            return [(gbuf[m % 2], b)]

        def whole(m):
            return self.qT[:, m, :] if m < 8 else self.kT[:, m - 8, :] if m < 16 else \
                self.vT[:, m - 16, :] if m < 24 else gbuf[m % 2]

        with nc.Block() as block:
            @block.sync
            def _(sp):
                sp.dma_start(wba, self.ins["w_ba"].rearrange("p (k m) -> p k m", k=KD)).then_inc(wba_in, 16)
                self.load_until(sp, w0 + 32)

            @block.tensor
            def _(pe):
                pe.wait_ge(wba_in, 16)
                for c in range(6):
                    src = self.hc[:, :, c * P:c * P + P] if c < 2 else self.h[:, :, (c - 2) * P:(c - 1) * P]
                    for k in range(KD):
                        mm = pe.matmul(self.bank[6][:, c * 32:c * 32 + 32], src[:, k, :], wba[:, k, :],
                                       start=(k == 0), stop=(k == KD - 1))
                mm.then_inc(ba_done, 1)
                for m in range(32):
                    w = self.tile(pe, w0 + m)
                    if m >= 3:
                        pe.wait_ge(taps if m < 27 else silu_done, m - 2)
                    if 8 <= m < 24:
                        self.project(pe, w, self.bank[3 + m % 3][:, 0:LC], self.hc)
                    self.project(pe, w, self.bank[m % 3][:, :], self.h).then_inc(self.w_done, 1)

            @block.scalar
            def _(act):
                def silu(m):
                    if m < 24:
                        act.wait_ge(taps, m + 1)
                        x = whole(m)
                        act.activation(x, x, ACT.Silu).then_inc(silu_done, 1)
                    else:
                        if m >= 26:
                            act.wait_ge(gate_out[m % 2], 16 * ((m - 24) // 2))
                        act.activation(gbuf[m % 2], self.bank[m % 3][:, :], ACT.Silu).then_inc(silu_done, 1)

                for m in range(24):
                    act.wait_ge(self.w_done, w0 + m + 1)
                    for dst, b in parts(m):
                        last = act.activation(dst, b, ACT.Copy, scale=conv[:, m, 2:3])
                    last.then_inc(centre, 1)
                    if m >= 1:
                        silu(m - 1)
                silu(23)
                for m in range(24, 32):
                    act.wait_ge(self.w_done, w0 + m + 1)
                    silu(m)

            @block.vector
            def _(dve):
                for m in range(24):
                    dve.wait_ge(centre, m + 1)
                    for j in [0, 1, 3, 4]:
                        for dst, b in parts(m):
                            n, s = dst.shape[1], j - 2
                            lo, hi = max(0, -s), n - max(0, s)
                            last = dve.scalar_tensor_tensor(dst[:, lo:hi], b[:, lo + s:hi + s], conv[:, m, j:j + 1],
                                                            dst[:, lo:hi], ALU.mult, ALU.add)
                        if j < 4:
                            self.dve.after(dve, last)
                    last.then_inc(taps, 1)
                dve.wait_ge(ba_done, 1)
                dve.tensor_copy(self.ba, self.bank[6][:, 0:192].rearrange("p (c j) -> p c j", c=6))

            @block.gpsimd
            def _(pool):
                for h in range(H):
                    pool.wait_ge(silu_done, 24 + h + 1)
                    pool.dma_start(self.gate_dram[:, h * L:(h + 1) * L], gbuf[h % 2]).then_inc(gate_out[h % 2], 16)
                for i in range(2):
                    pool.wait_ge(gate_out[i], 16 * H // 2)

    def gdn_prepare(self):
        nc = self.nc
        f = self.g_free
        sq = [self.cols(f + 768 * i, 768) for i in range(2)]
        gt = lambda i: self.view(f + 1536 + 96 * i, 6, 16)
        self.beta, self.negs, self.ee, self.g, self.gate_sum = gt(0), gt(1), gt(2), gt(3), gt(4)
        t0, t1, t2 = gt(5), gt(6), gt(7)
        assert 1536 + 9 * 96 <= 2560
        self.core_free = f + 1536 + 5 * 96
        self.a_rows = gt(8)
        ba = self.ba.rearrange("p c (d w h) -> p c d w h", d=2, w=2)
        squares, sums = self.sem("qk_squares"), self.sem("qk_sums")
        rstd, scaled = self.sem("qk_rstd"), self.sem("qk_scaled")
        turned, kept = self.sem("kv_turned"), self.sem("kv_kept")
        g1, g2, g3, g4 = self.sem("gate_in"), self.sem("gate_act"), self.sem("gate_sums"), self.sem("gate_gc")

        def job(j):
            if j < 8:
                return self.qT[:, j, :], [(self.bank[j % 2][:, :], slice(0, L))]
            return self.kT[:, j - 8, :], [(self.bank[2 + j % 2][:, 0:LC], slice(0, LC)),
                                          (self.bank[j % 2][:, :], slice(LC, LC + L))]

        turns = [(src, dst, c, g) for src, dst in ((self.vT, self.vnat), (self.kT, self.knat))
                 for c in range(6) for g in range(2)]
        with nc.Block() as block:
            @block.scalar
            def _(act):
                act.wait_ge(g1, 1)
                act.activation(self.beta, t0, ACT.Sigmoid).then_inc(g2, 1)
                self.act.after(act, act.activation(t2, t2, ACT.Exp, scale=-1.0))
                act.activation(t2, t2, ACT.Ln, bias=1.0).then_inc(g2, 1)
                act.activation(self.gate_sum, self.a_rows, ACT.Exp).then_inc(g2, 1)

                def rstds(j):
                    act.wait_ge(sums, j + 1)
                    x, parts = job(j)
                    for b, cols in parts:
                        last = act.activation(sq[j % 2][:, cols], b, ACT.Ln, bias=self.C("eps"))
                    self.act.after(act, last)
                    n = x.shape[1]
                    if j < 8:
                        act.activation(sq[j % 2][:, 0:n], sq[j % 2][:, 0:n], ACT.Exp, scale=-0.5,
                                       bias=self.C("ln_dk")).then_inc(rstd, 1)
                    else:
                        act.activation(sq[j % 2][:, 0:n], sq[j % 2][:, 0:n], ACT.Exp, scale=-0.5).then_inc(rstd, 1)

                for j in range(16):
                    x, _ = job(j)
                    if j >= 2:
                        act.wait_ge(scaled, j - 1)
                    act.activation(sq[j % 2][:, 0:x.shape[1]], x, ACT.Square).then_inc(squares, 1)
                    if j >= 1:
                        rstds(j - 1)
                rstds(15)
                act.wait_ge(g3, 1)
                act.wait_ge(g4, 2)
                act.activation(t1, t1, ACT.Exp).then_inc(g2, 1)
                act.activation(self.ee, self.ee, ACT.Exp).then_inc(g2, 1)

            @block.tensor
            def _(pe):
                for n, (src, dst, c, g) in enumerate(turns[:12]):
                    if n >= 2:
                        pe.wait_ge(kept, n - 1)
                    for i in range(4):
                        mm = pe.transpose(self.bank[4 + n % 2][:, i * P:(i + 1) * P],
                                          src[:, 4 * g + i, c * P:(c + 1) * P], self.C("ident"))
                    mm.then_inc(turned, 1)
                for j in range(16):
                    pe.wait_ge(squares, j + 1)
                    if j >= 2:
                        pe.wait_ge(rstd, j - 1)
                    for b, cols in job(j)[1]:
                        mm = pe.matmul(b, self.C("ones"), sq[j % 2][:, cols], start=True, stop=True)
                    mm.then_inc(sums, 1)
                pe.wait_ge(g3, 1)
                for d, tri in enumerate(["tri_f", "tri_b"]):
                    for c in range(6):
                        pe.matmul(self.bank[6][:, c * 16 + 8 * d:c * 16 + 8 * d + 8], self.C(tri),
                                  self.g[:, c, 8 * d:8 * d + 8], start=True, stop=True)
                pe.matmul(self.bank[7][:, 0:96], self.C("ones"), self.g.rearrange("p a b -> p (a b)"),
                          start=True, stop=True).then_inc(g4, 1)
                for n, (src, dst, c, g) in list(enumerate(turns))[12:]:
                    pe.wait_ge(kept, n - 1)
                    pe.wait_ge(scaled, 16)
                    for i in range(4):
                        mm = pe.transpose(self.bank[4 + n % 2][:, i * P:(i + 1) * P],
                                          src[:, 4 * g + i, c * P:(c + 1) * P], self.C("ident"))
                    mm.then_inc(turned, 1)

            @block.vector
            def _(dve):
                for c in range(6):
                    for d in range(2):
                        dve.tensor_copy(t0[:, c, 8 * d:8 * d + 8], ba[:, c, d, 0, :])
                        last = dve.tensor_tensor(t1[:, c, 8 * d:8 * d + 8], ba[:, c, d, 1, :],
                                                 self.S("dt", 8 * d, 8 * d + 8), ALU.add)
                self.dve.after(dve, last)
                dve.tensor_copy(self.a_rows, self.S("a_log").rearrange("p (a b) -> p a b", a=1).to_broadcast([P, 6, 16]))
                self.dve.after(dve, dve.tensor_scalar(t2, t1, -1.0, None, ALU.mult))
                dve.tensor_tensor(t2, t2, t1, ALU.max).then_inc(g1, 1)
                dve.wait_ge(g2, 3)
                self.dve.after(dve, dve.scalar_tensor_tensor(t1, t1, 0.0, t2, ALU.max, ALU.add))
                dve.scalar_tensor_tensor(self.g, t1, -1.0, self.gate_sum, ALU.mult, ALU.mult).then_inc(g3, 1)

                def keep(n):
                    src, dst, c, g = turns[n]
                    dve.wait_ge(turned, n + 1)
                    dve.tensor_copy(dst[:, c, 512 * g:512 * g + 512], self.bank[4 + n % 2][:, :]).then_inc(kept, 1)

                for n in range(12):
                    keep(n)
                for j in range(16):
                    x, _ = job(j)
                    dve.wait_ge(rstd, j + 1)
                    dve.tensor_tensor(x, x, sq[j % 2][:, 0:x.shape[1]], ALU.mult).then_inc(scaled, 1)
                dve.wait_ge(g4, 1)
                gc = self.bank[6][:, 0:96].rearrange("p (a b) -> p a b", a=6)
                total = self.bank[7][:, 0:96].rearrange("p (a b) -> p a b", a=6)
                dve.tensor_copy(self.gate_sum, gc)
                self.dve.after(dve, dve.tensor_copy(t1, gc))
                dve.tensor_tensor(self.ee, total, t1, ALU.subtract).then_inc(g4, 1)
                dve.wait_ge(g2, 5)
                dve.scalar_tensor_tensor(self.negs, t1, -1.0, self.beta, ALU.mult, ALU.mult)
                for n in range(12, 24):
                    keep(n)

    def gdn_core(self):
        nc = self.nc
        f = self.core_free
        S = self.view(f, 2 * H, P)
        f += 2 * H * P
        names = ["dt", "er", "pt", "qd", "xs", "zs", "vn", "kd", "r"]
        buf = [{n: self.view(f + (u * len(names) + i) * 512, 4, P) for i, n in enumerate(names)} for u in range(2)]
        f += 2 * len(names) * 512
        for b in buf:
            b["b"] = b["dt"]
            b["yn"] = b["r"][:, 0:2, :]
            b["bl"] = b["r"][:, 2:4, :]
            b["xl"] = b["xs"].rearrange("p (t q) c -> p t q c", t=2)
        acc = [self.cols(f + P * i, P) for i in range(4)]
        f += 4 * P
        cond = self.cols(f, 24)
        c1, c2 = cond[:, 0:16].rearrange("p (k s) -> p k s", k=KD), cond[:, 16:24].rearrange("p (k s) -> p k s", k=KD)
        assert f + 24 <= self.total, (f, self.total)
        oT = self.x
        ident = self.C("ident")
        ident4 = ident.rearrange("p (a b) -> p a b", a=1).to_broadcast([P, 4, P])
        bank = lambda b: self.bank[b][:, :].rearrange("p (a b) -> p a b", a=4)
        X, Z, Y, M = [bank(0), bank(1)], [bank(2), bank(3)], [bank(4), bank(5)], [bank(6), bank(7)]
        pairs = [(s, g) for s in range(6) for g in range(2)]
        order = [[0, 1, 2, 3, 4, 5], [1, 0, 5, 4, 3, 2]]
        levels = self.C("levels").rearrange("p (l a b) -> p l a b", l=6, a=1)
        first = [self.C(n).rearrange("p (a b) -> p a b", a=1).to_broadcast([P, 4, P]) for n in ("pair_f", "pair_b")]
        tri, neg = [self.C("tri_f"), self.C("tri_b")], [self.C("neg_f"), self.C("neg_b")]
        s = {n: self.sem("core_" + n) for n in
             ["rows", "gram", "qk", "min", "exp", "er", "pre", "b", "pt", "z0", "y", "yn", "x", "xs", "z", "zs",
              "ks", "r", "v", "vs", "oadd", "su", "sm", "s", "zero", "cond", "modc", "prod", "modm", "bl", "blank"]}
        w0 = TILE0["mod2"]
        fill = [11] * 8 + [10] * 4
        assert sum(fill) == 128

        def fills(p, l):
            return range(sum(fill[:p]) + 2 * (l - 1), sum(fill[:p]) + min(2 * l, fill[p]))

        def col(a, u, g, c):
            base = 8 * u + 4 * g
            return a[:, c, base:base + 4].rearrange("p (h o) -> p h o", o=1).to_broadcast([P, 4, P])

        def touched(a, l, side):
            b = 1 << l
            return a.rearrange("p a (n t b) -> p a n t b", t=2, b=b)[:, :, :, side, :]

        def gathered(a, l):
            return a.rearrange("p q (h n b) -> p (q h) n b", h=2, b=1 << l)

        with nc.Block() as block:
            @block.sync
            def _(sp):
                sp.wait_ge(s["zero"], 1)
                self.blank_spare_rows(sp, oT[:, 0:2, :], s["blank"])
                self.load_until(sp, w0 + 128)

            @block.tensor
            def _(pe):
                pe.wait_ge(s["zero"], 1)
                pe.wait_ge(s["cond"], 1)

                def mod_sums(p, l):
                    for i in fills(p, l):
                        pe.wait_ge(self.w_done, w0 + i + 1)
                        j = i - sum(fill[:p])
                        pe.matmul(M[1][:, 0, j:j + 1], acc[i % 4], self.C("ones")[:, 0:1],
                                  start=True, stop=True).then_inc(s["modm"], 1)

                for p, (st, g) in enumerate(pairs):
                    for u in range(2):
                        c = order[u][st]
                        cols = slice(c * P, c * P + P)
                        if p >= 1:
                            pe.wait_ge(s["s"], 2 * (p - 1) + u + 1)
                            pe.wait_ge(s["oadd"], 2 * (p - 1) + u + 1)
                        for h in range(4):
                            gcol = self.g[:, c, 8 * u + 4 * g + h:8 * u + 4 * g + h + 1].to_broadcast([P, P])
                            mm = pe.matmul(X[u][:, h, :], gcol, tri[u], start=True, stop=True)
                        mm.then_inc(s["rows"], 1)
                        for h in range(4):
                            bcol = self.beta[:, c, 8 * u + 4 * g + h:8 * u + 4 * g + h + 1].to_broadcast([P, P])
                            pe.matmul(Z[u][:, h, :], bcol, ident, start=True, stop=True)
                        for h in range(4):
                            k = self.kT[:, 4 * g + h, cols]
                            mm = pe.matmul(Y[u][:, h, :], k, k, start=True, stop=True)
                        mm.then_inc(s["gram"], 1)
                        if st >= 2:
                            for h in range(4):
                                mm = pe.matmul(M[u][:, h, :], self.kT[:, 4 * g + h, cols],
                                               self.qT[:, 4 * g + h, (c - 2) * P:(c - 1) * P], start=True, stop=True)
                            mm.then_inc(s["qk"], 1)
                    for u in range(2):
                        pe.wait_ge(s["z0"], 2 * p + u + 1)
                        for h in range(4):
                            mm = pe.matmul(X[u][:, h, :], buf[u]["zs"][:, h, :], ident, is_transpose=True,
                                           start=(h == 0), stop=False, skip_group_check=True)
                        mm.then_inc(s["x"], 1)
                    for l in range(1, 7):
                        for u in range(2):
                            pe.wait_ge(s["xs"], 14 * p + 2 * (l - 1) + u + 1)
                            pe.wait_ge(s["bl"], 12 * p + 2 * (l - 1) + u + 1)
                            for q in range(2):
                                mm = pe.matmul(Y[u][:, q, :], buf[u]["bl"][:, q, :], buf[u]["xl"][:, u, q, :],
                                               start=True, stop=True)
                            mm.then_inc(s["y"], 1)
                            for q in range(2):
                                mm = pe.transpose(Z[u][:, q, :], buf[u]["xl"][:, 1 - u, q, :], ident)
                            mm.then_inc(s["z"], 1)
                        if l > 1:
                            mod_sums(p, l - 1)
                        for u in range(2):
                            pe.wait_ge(s["yn"], 12 * p + 2 * (l - 1) + u + 1)
                            pe.wait_ge(s["zs"], 14 * p + 2 * (l - 1) + u + 1)
                            for q in range(2):
                                mm = pe.matmul(touched(X[u][:, 2 * q:2 * q + 2, :], l, u), buf[u]["zs"][:, q, :],
                                               buf[u]["yn"][:, q, :], start=False, stop=(l == 6), skip_group_check=True)
                            mm.then_inc(s["x"], 1)
                    mod_sums(p, 6)
                    for u in range(2):
                        c, base = order[u][st], 8 * u + 4 * g
                        pe.wait_ge(s["xs"], 14 * p + 12 + u + 1)
                        for h in range(4):
                            mm = pe.transpose(Z[u][:, h, :], buf[u]["xs"][:, h, :], ident)
                        mm.then_inc(s["z"], 1)
                        for h in range(4):
                            mm = pe.matmul(X[u][:, h, :], self.kT[:, 4 * g + h, c * P:c * P + P], S[:, base + h, :],
                                           start=True, stop=True)
                        mm.then_inc(s["ks"], 1)
                    for u in range(2):
                        pe.wait_ge(s["r"], 2 * p + u + 1)
                        pe.wait_ge(s["zs"], 14 * p + 12 + u + 1)
                        for h in range(4):
                            mm = pe.matmul(Y[u][:, h, :], buf[u]["zs"][:, h, :], buf[u]["r"][:, h, :],
                                           start=True, stop=True)
                        mm.then_inc(s["v"], 1)
                    for u in range(2):
                        base = 8 * u + 4 * g
                        vn = buf[u]["vn"]
                        pe.wait_ge(s["vs"], 2 * p + u + 1)
                        pe.wait_ge(s["pre"], 2 * p + u + 1)
                        for h in range(4):
                            mm = pe.matmul(Z[u][:, h, :], buf[u]["kd"][:, h, :], vn[:, h, :], start=True, stop=True)
                        if u == 1:
                            pe.wait_ge(s["modc"], p + 1)
                        if st >= 2:
                            for h in range(4):
                                pe.matmul(M[u][:, h, :], S[:, base + h, :], buf[u]["qd"][:, h, :], start=True, stop=False)
                                mm = pe.matmul(M[u][:, h, :], vn[:, h, :], buf[u]["pt"][:, h, :], start=False, stop=True)
                        mm.then_inc(s["su"], 1)

            @block.scalar
            def _(act):
                def gather_b(u, l):
                    act.activation(gathered(buf[u]["bl"], l), touched(buf[u]["b"], l, 1 - u), ACT.Copy).then_inc(s["bl"], 1)

                act.activation(c1, self.S("c1").rearrange("p (k s) -> p k s", k=KD), ACT.Silu)
                act.activation(c2, self.S("c2").rearrange("p (k s) -> p k s", k=KD), ACT.Silu).then_inc(s["cond"], 1)
                for p, (st, g) in enumerate(pairs):
                    for u in range(2):
                        act.wait_ge(s["rows"], 2 * p + u + 1)
                        act.activation(buf[u]["er"], X[u], ACT.Exp).then_inc(s["er"], 1)
                    for u in range(2):
                        act.wait_ge(s["min"], 2 * p + u + 1)
                        act.activation(buf[u]["dt"], buf[u]["dt"], ACT.Exp).then_inc(s["exp"], 1)
                    for u in range(2):
                        act.wait_ge(s["z0"], 2 * p + u + 1)
                        gather_b(u, 1)
                    for l in range(7):
                        for u in range(2):
                            act.wait_ge(s["x"], 14 * p + 2 * l + u + 1)
                            if l == 6:
                                act.activation(buf[u]["xs"], X[u], ACT.Copy).then_inc(s["xs"], 1)
                                continue
                            for side in range(2):
                                ins = act.activation(gathered(buf[u]["xl"][:, side, :, :], l + 1), touched(X[u], l + 1, side),
                                                     ACT.Copy)
                            ins.then_inc(s["xs"], 1)
                        for u in range(2):
                            act.wait_ge(s["z"], 14 * p + 2 * l + u + 1)
                            n = 2 if l < 6 else 4
                            act.activation(buf[u]["zs"][:, 0:n, :], Z[u][:, 0:n, :], ACT.Copy).then_inc(s["zs"], 1)
                        for u in range(2):
                            if l < 5:
                                act.wait_ge(s["y"], 12 * p + 2 * l + u + 1)
                                gather_b(u, l + 2)
                    for u in range(2):
                        act.wait_ge(s["v"], 2 * p + u + 1)
                        act.activation(buf[u]["vn"], Y[u], ACT.Copy).then_inc(s["vs"], 1)

            @block.gpsimd
            def _(pool):
                pool.wait_ge(s["cond"], 1)
                pool.memset(oT, 0.0)
                pool.memset(S, 0.0).then_inc(s["zero"], 1)
                for p, (st, g) in enumerate(pairs):
                    for u in range(2):
                        b, c = buf[u], order[u][st]
                        pool.wait_ge(s["er"], 2 * p + u + 1)
                        pool.tensor_tensor(b["kd"], self.knat[:, c, 512 * g:512 * g + 512].rearrange("p (a b) -> p a b", a=4),
                                           col(self.ee, u, g, c), ALU.mult)
                        if st >= 2:
                            pool.tensor_tensor(b["qd"], self.qT[:, 4 * g:4 * g + 4, (c - 2) * P:(c - 1) * P], b["er"], ALU.mult)
                        pool.tensor_tensor(b["vn"], self.vnat[:, c, 512 * g:512 * g + 512].rearrange("p (a b) -> p a b", a=4),
                                           col(self.beta, u, g, c), ALU.mult).then_inc(s["pre"], 1)
                    for l in range(1, 7):
                        for i in fills(p, l):
                            w = self.tile(pool, w0 + i)
                            src = c1[:, :, 0:1] if i < 32 else c2
                            pool.tensor_tensor(w, w, src.to_broadcast([P, KD, P]), ALU.mult).then_inc(s["prod"], 1)
                    for u in range(2):
                        base = 8 * u + 4 * g
                        last = P - 1 if u == 0 else 0
                        pool.wait_ge(s["su"], 2 * p + u + 1)
                        pool.tensor_tensor(S[:, base:base + 4, :], S[:, base:base + 4, :],
                                           buf[u]["er"][:, :, last:last + 1].to_broadcast([P, 4, P]), ALU.mult).then_inc(s["sm"], 1)

            @block.vector
            def _(dve):
                dve.wait_ge(s["zero"], 1)
                for p, (st, g) in enumerate(pairs):
                    for u in range(2):
                        dve.wait_ge(s["er"], 2 * p + u + 1)
                        self.dve.after(dve, dve.tensor_tensor(buf[u]["dt"], X[u], col(self.gate_sum, u, g, order[u][st]), ALU.subtract))
                        dve.tensor_tensor(buf[u]["dt"], buf[u]["dt"], neg[u].rearrange("p (a b) -> p a b", a=1).to_broadcast([P, 4, P]),
                                          ALU.min).then_inc(s["min"], 1)
                    for u in range(2):
                        b = buf[u]
                        dve.wait_ge(s["exp"], 2 * p + u + 1)
                        dve.wait_ge(s["gram"], 2 * p + u + 1)
                        if st >= 2:
                            dve.wait_ge(s["qk"], 2 * (p - 4) + u + 1)
                            dve.tensor_tensor(b["pt"], b["dt"], M[u], ALU.mult).then_inc(s["pt"], 1)
                        self.dve.after(dve, dve.tensor_tensor(b["b"], b["dt"], Z[u], ALU.mult))
                        self.dve.after(dve, dve.tensor_tensor(b["b"], b["b"], Y[u], ALU.mult))
                        self.dve.after(dve, dve.tensor_tensor(b["zs"], b["b"], first[u], ALU.mult))
                        dve.tensor_tensor(b["zs"], b["zs"], ident4, ALU.add).then_inc(s["z0"], 1)
                    for l in range(1, 7):
                        for u in range(2):
                            dve.wait_ge(s["y"], 12 * p + 2 * (l - 1) + u + 1)
                            dve.tensor_tensor(buf[u]["yn"], Y[u][:, 0:2, :], levels[:, l - 1, :, :].to_broadcast([P, 2, P]),
                                              ALU.mult).then_inc(s["yn"], 1)
                        for i in fills(p, l):
                            dve.wait_ge(s["prod"], i + 1)
                            if i >= 4:
                                dve.wait_ge(s["modm"], i - 3)
                            w = self.ring[:, (w0 + i) % RING, :].rearrange("p (k m) -> p m k", k=KD)
                            dve.tensor_reduce(acc[i % 4], w, AX.X, ALU.add).then_inc(self.w_done, 1)
                    f1 = sum(fill[:p + 1])
                    dve.wait_ge(s["modm"], f1)
                    at = 16 + f1 - fill[p]
                    dve.tensor_tensor(self.mod_all[:, at:at + fill[p]], M[1][:, 0, 0:fill[p]],
                                      self.S("mod_b", at, at + fill[p]), ALU.add).then_inc(s["modc"], 1)
                    for u in range(2):
                        b, c = buf[u], order[u][st]
                        dve.wait_ge(s["ks"], 2 * p + u + 1)
                        self.dve.after(dve, dve.tensor_tensor(b["r"], X[u], col(self.negs, u, g, c), ALU.mult))
                        dve.wait_ge(s["pre"], 2 * p + u + 1)
                        dve.tensor_tensor(b["r"], b["r"], b["vn"], ALU.add).then_inc(s["r"], 1)
                    for u in range(2):
                        c, base = order[u][st], 8 * u + 4 * g
                        dve.wait_ge(s["su"], 2 * p + u + 1)
                        if p == 4 and u == 0:
                            dve.wait_ge(s["blank"], 16 * OVF)
                        if st >= 2:
                            o = oT[:, 4 * g:4 * g + 4, (c - 2) * P:(c - 1) * P]
                            dve.tensor_tensor(o, o, M[u], ALU.add).then_inc(s["oadd"], 1)
                        else:
                            dve.engine_nop().then_inc(s["oadd"], 1)
                        dve.wait_ge(s["sm"], 2 * p + u + 1)
                        dve.tensor_tensor(S[:, base:base + 4, :], S[:, base:base + 4, :], Z[u], ALU.add).then_inc(s["s"], 1)
                    dve.wait_ge(s["oadd"], 2 * (p + 1))

    def gdn_finish(self):
        nc = self.nc
        f = self.free0
        o = self.view(f, H, L)
        gate = self.view(f + H * L, H, L)
        rs = [self.cols(f + 2 * H * L + 512 * i, 512) for i in range(2)]
        gate_in, x_in = self.sem("gate_loaded"), self.sem("x_reloaded")
        sq, ss, r, nd = (self.sem("o_" + n) for n in ["squares", "sums", "rstd", "normed"])
        w0 = TILE0["gdn_out"]
        with nc.Block() as block:
            @block.sync
            def _(sp):
                sp.dma_start(gate, self.gate_dram.rearrange("p (h t) -> p h t", h=H)).then_inc(gate_in, 16)
                sp.wait_ge(nd, H)
                sp.dma_start(self.x, self.ins["xT"].rearrange("p (k t) -> p k t", k=KD)).then_inc(x_in, 16)
                self.load_until(sp, w0 + 8)

            @block.scalar
            def _(act):
                for h in range(H):
                    act.activation(o[:, h, :], self.x[:, h, :], ACT.Square).then_inc(sq, 1)
                for h in range(H):
                    act.wait_ge(ss, h + 1)
                    if h >= 2:
                        act.wait_ge(nd, h - 1)
                    self.act.after(act, act.activation(rs[h % 2], self.bank[h % 2][:, :], ACT.Ln, scale=1.0 / P,
                                                       bias=self.C("eps")))
                    act.activation(rs[h % 2], rs[h % 2], ACT.Exp, scale=-0.5).then_inc(r, 1)

            @block.vector
            def _(dve):
                dve.wait_ge(gate_in, 16)
                for h in range(H):
                    dve.wait_ge(r, h + 1)
                    self.dve.after(dve, dve.scalar_tensor_tensor(o[:, h, :], self.x[:, h, :], self.S("gdn_norm"),
                                                                 rs[h % 2], ALU.mult, ALU.mult))
                    dve.tensor_tensor(o[:, h, :], o[:, h, :], gate[:, h, :], ALU.mult).then_inc(nd, 1)
                dve.wait_ge(x_in, 16)
                self.residual(dve, w0, self.mod["lat"][:, 16:24])

            @block.tensor
            def _(pe):
                for h in range(H):
                    pe.wait_ge(sq, h + 1)
                    if h >= 2:
                        pe.wait_ge(r, h - 1)
                    pe.matmul(self.bank[h % 2][:, :], self.C("ones"), o[:, h, :], start=True, stop=True).then_inc(ss, 1)
                pe.wait_ge(nd, H)
                self.out_projection(pe, w0, o)

    def out_projection(self, pe, w0, src):
        done = self.sem("residual_added")
        for m in range(KD):
            w = self.tile(pe, w0 + m)
            if m >= 4:
                pe.wait_ge(done, self.residuals + m - 3)
            self.project(pe, w, self.bank[m % 4][:, :], src).then_inc(self.w_done, 1)

    residuals = 0

    def residual(self, dve, w0, gate):
        done = self.sem("residual_added")
        for m in range(KD):
            dve.wait_ge(self.w_done, w0 + m + 1)
            dve.scalar_tensor_tensor(self.x[:, m, :], self.bank[m % 4][:, :], gate[:, m:m + 1], self.x[:, m, :],
                                     ALU.mult, ALU.add).then_inc(done, 1)

    def ffn(self):
        nc = self.nc
        f = self.free0
        h = self.view(f, KD, L)
        a = self.view(f + KD * L, KF, L)
        f += KD * L + KF * L
        cv = [self.cols(f + 512 * i, 512) for i in range(2)]
        e = [self.cols(f + 1024 + 512 * i, 512) for i in range(2)]
        w0, w1 = TILE0["ffn_in"], TILE0["ffn_out"]
        taps = self.S("fconv").rearrange("p (m j) -> p m j", m=KF)
        centre, conv, silus, acts = (self.sem("ffn_" + n) for n in ["centre", "conv", "silu", "act"])
        with nc.Block() as block:
            @block.sync
            def _(sp):
                self.load_until(sp, w1 + KF)

            @block.tensor
            def _(pe):
                for m in range(KF):
                    if m >= 3:
                        pe.wait_ge(acts, m - 2)
                    for i in range(2):
                        w = self.tile(pe, w0 + 2 * m + i)
                        self.project(pe, w, self.bank[2 * (m % 3) + i][:, :], h).then_inc(self.w_done, 1)
                for m in range(KF):
                    pe.wait_ge(acts, KF)
                    w = self.tile(pe, w1 + m)
                    for k in range(KD):
                        mm = pe.matmul(self.bank[k][:, :], w[:, k, :], a[:, m, :], start=(m == 0), stop=(m == KF - 1))
                    mm.then_inc(self.w_done, 1)

            @block.scalar
            def _(act):
                def silu(m):
                    act.wait_ge(conv, m + 1)
                    if m >= 2:
                        act.wait_ge(acts, m - 1)
                    act.activation(e[m % 2], cv[m % 2], ACT.Silu).then_inc(silus, 1)

                for m in range(KF):
                    act.wait_ge(self.w_done, w0 + 2 * m + 2)
                    if m >= 2:
                        act.wait_ge(acts, m - 1)
                    act.activation(cv[m % 2], self.bank[2 * (m % 3) + 1][:, :], ACT.Identity, scale=taps[:, m, 1:2],
                                   bias=self.S("fconv_b", m, m + 1)).then_inc(centre, 1)
                    if m >= 1:
                        silu(m - 1)
                silu(KF - 1)

            @block.vector
            def _(dve):
                def glu(m):
                    dve.wait_ge(silus, m + 1)
                    dve.tensor_tensor(a[:, m, :], e[m % 2], self.bank[2 * (m % 3)][:, :], ALU.mult).then_inc(acts, 1)

                for m in range(KF):
                    dve.wait_ge(centre, m + 1)
                    b, x = self.bank[2 * (m % 3) + 1], cv[m % 2]
                    self.dve.after(dve, dve.scalar_tensor_tensor(x[:, 1:L], b[:, 0:L - 1], taps[:, m, 0:1], x[:, 1:L],
                                                                 ALU.mult, ALU.add))
                    dve.scalar_tensor_tensor(x[:, 0:L - 1], b[:, 1:L], taps[:, m, 2:3], x[:, 0:L - 1],
                                             ALU.mult, ALU.add).then_inc(conv, 1)
                    if m >= 1:
                        glu(m - 1)
                glu(KF - 1)
                dve.wait_ge(self.w_done, w1 + KF)
                for k in range(KD):
                    dve.scalar_tensor_tensor(self.x[:, k, :], self.bank[k][:, :], self.mod["lat"][:, 40 + k:41 + k],
                                             self.x[:, k, :], ALU.mult, ALU.add)

    def project_all(self, name, w0, dsts, src, extra=None):
        nc = self.nc
        even, odd = self.sem(name + "_even_kept"), self.sem(name + "_odd_kept")
        with nc.Block() as block:
            @block.sync
            def _(sp):
                self.load_until(sp, w0 + len(dsts))

            @block.tensor
            def _(pe):
                for m in range(len(dsts)):
                    w = self.tile(pe, w0 + m)
                    if m >= 4:
                        pe.wait_ge([even, odd][m % 2], (m - 4) // 2 + 1)
                    self.project(pe, w, self.bank[m % 4][:, :], src).then_inc(self.w_done, 1)

            @block.scalar
            def _(act):
                for m in range(0, len(dsts), 2):
                    act.wait_ge(self.w_done, w0 + m + 1)
                    act.activation(dsts[m], self.bank[m % 4][:, :], ACT.Copy).then_inc(even, 1)

            @block.vector
            def _(dve):
                for m in range(1, len(dsts), 2):
                    dve.wait_ge(self.w_done, w0 + m + 1)
                    dve.tensor_copy(dsts[m], self.bank[m % 4][:, :]).then_inc(odd, 1)

    def head_norms(self, name, jobs, ones, width, scratch):
        nc = self.nc
        sq, ss, r, nd = (self.sem(name + n) for n in ["_squares", "_sums", "_rstd", "_normed"])
        t = [self.cols(scratch + 512 * i, 512) for i in range(4)]
        with nc.Block() as block:
            @block.scalar
            def _(act):
                def rstd(j):
                    act.wait_ge(ss, j + 1)
                    if j >= 2:
                        act.wait_ge(nd, j - 1)
                    self.act.after(act, act.activation(t[2 + j % 2], self.bank[j % 2][:, :], ACT.Ln, scale=1.0 / width,
                                                       bias=self.C("eps")))
                    act.activation(t[2 + j % 2], t[2 + j % 2], ACT.Exp, scale=-0.5).then_inc(r, 1)

                for j, (x, gain, factor) in enumerate(jobs):
                    if j >= 2:
                        act.wait_ge(ss, j - 1)
                    act.activation(t[j % 2], x, ACT.Square).then_inc(sq, 1)
                    if j >= 1:
                        rstd(j - 1)
                rstd(len(jobs) - 1)

            @block.tensor
            def _(pe):
                for j in range(len(jobs)):
                    pe.wait_ge(sq, j + 1)
                    if j >= 2:
                        pe.wait_ge(r, j - 1)
                    pe.matmul(self.bank[j % 2][:, :], self.C(ones), t[j % 2], start=True, stop=True).then_inc(ss, 1)

            @block.vector
            def _(dve):
                for j, (x, gain, factor) in enumerate(jobs):
                    dve.wait_ge(r, j + 1)
                    last = dve.scalar_tensor_tensor(x, x, gain, t[2 + j % 2], ALU.mult, ALU.mult)
                    if factor is not None:
                        self.dve.after(dve, last)
                        last = dve.tensor_tensor(x, x, factor, ALU.mult)
                    last.then_inc(nd, 1)

    def turn_all(self, name, groups):
        nc = self.nc
        turned, even, odd = self.sem(name + "_turned"), self.sem(name + "_even_kept"), self.sem(name + "_odd_kept")
        with nc.Block() as block:
            @block.tensor
            def _(pe):
                for n, (srcs, dst) in enumerate(groups):
                    if n >= 4:
                        pe.wait_ge([even, odd][n % 2], (n - 4) // 2 + 1)
                    for i, src in enumerate(srcs):
                        mm = pe.transpose(self.bank[n % 4][:, i * P:(i + 1) * P], src, self.C("ident"))
                    mm.then_inc(turned, 1)

            @block.scalar
            def _(act):
                for n in range(0, len(groups), 2):
                    act.wait_ge(turned, n + 1)
                    act.activation(groups[n][1], self.bank[n % 4][:, :].rearrange("p (a b) -> p a b", a=4), ACT.Copy).then_inc(even, 1)

            @block.vector
            def _(dve):
                for n in range(1, len(groups), 2):
                    dve.wait_ge(turned, n + 1)
                    dve.tensor_copy(groups[n][1], self.bank[n % 4][:, :].rearrange("p (a b) -> p a b", a=4)).then_inc(odd, 1)

    def project_out(self, name, w0, src, gate):
        nc = self.nc
        with nc.Block() as block:
            @block.sync
            def _(sp):
                self.load_until(sp, w0 + KD)

            @block.tensor
            def _(pe):
                self.out_projection(pe, w0, src)

            @block.vector
            def _(dve):
                self.residual(dve, w0, gate)
        self.residuals += KD

    def band_bias(self, band, hankel):
        nc = self.nc
        row = self.cols(self.total - BAND_LEN, BAND_LEN)
        made, kept, stored, spread, turned = (self.sem("band_" + n) for n in
                                              ["made", "kept", "stored", "spread", "turned"])
        flat = [a.rearrange("p a b -> p (a b)") for a in (band, hankel)]
        with nc.Block() as block:
            @block.tensor
            def _(pe):
                pe.matmul(self.bank[0][0:H, 0:BAND_LEN], self.S("rel")[0:32, :], self.C("bucket")[0:32, :],
                          start=True, stop=True).then_inc(made, 1)
                pe.wait_ge(spread, 16)
                for i in range(4):
                    pe.matmul(self.bank[1 + i][:, :], self.C("flip"), flat[1][:, 512 * i:512 * i + 512],
                              start=True, stop=True).then_inc(turned, 1)

            @block.vector
            def _(dve):
                dve.wait_ge(made, 1)
                dve.tensor_copy(row[0:H, :], self.bank[0][0:H, 0:BAND_LEN]).then_inc(kept, 1)
                for i in range(4):
                    dve.wait_ge(turned, i + 1)
                    dve.tensor_copy(flat[0][:, 512 * i:512 * i + 512], self.bank[1 + i][:, :])

            @block.scalar
            def _(act):
                act.wait_ge(kept, 1)
                act.dma_start(self.band_dram[:, :], row[0:H, :]).then_inc(stored, 16)
                act.wait_ge(stored, 16)
                src = bass.AP(self.band_dram[:, :].tensor, 0, [[1, P], [BAND_LEN, H], [1, 2 * P]])
                act.dma_start(hankel, src).then_inc(spread, 16)

    def even_mixer(self):
        f = self.free0
        h = self.view(f, KD, L)
        f += KD * L
        qa, ka, va = self.view(f, 4, L), self.view(f + 2048, 1, L), self.view(f + 2560, 4, P)
        f += 3072
        qb, kb = self.view(f, 2, L), self.view(f + 1024, 2, L)
        rb, vb = self.view(f + 2048, 4, L), self.view(f + 4096, 4, L)
        f += 6144
        band = self.view(f, H, 2 * P)
        f += 2048
        o = self.view(f, KD, L)
        f += KD * L
        free = f
        vaT, vbT = self.view(free, 1, L), self.view(free + 512, 4, L)
        w0 = TILE0["even_in"]
        dsts = [qa[:, i, :] for i in range(4)] + [ka[:, 0, :], vaT[:, 0, :]] + [qb[:, i, :] for i in range(2)] + \
            [kb[:, i, :] for i in range(2)] + [vbT[:, i, :] for i in range(4)] + [rb[:, i, :] for i in range(4)]
        self.project_all("even", w0, dsts, h)
        blk = lambda a, i: a[:, i * P:(i + 1) * P]
        self.turn_all("even_v", [([blk(vaT[:, 0, :], b) for b in range(4)], va)] +
                      [([blk(vbT[:, i, :], b) for i in range(4)], vb[:, b, :].rearrange("p (a b) -> p a b", a=4))
                       for b in range(4)])
        self.head_norms("a_qk", [(qa[:, i, :], self.S("a_q"), None) for i in range(4)] +
                        [(ka[:, 0, :], self.S("a_k"), None)], "ones64", 64, free)
        self.gla_gates(h, qb, kb, rb, free)
        self.swa_band = self.view(free + 4096 + 4096 + 64, H, 2 * P)
        self.band_bias(band, self.swa_band)
        self.swa(qa, ka, va, band, o, free + 4096)
        self.gla(vb, o, free)
        self.head_norms("b_out", [(o[:, 4 + i, :], self.S("b_norm"), rb[:, i, :]) for i in range(4)], "ones", P, free)
        self.project_out("even_out", TILE0["even_out"], o, self.mod["even"][:, 16:24])

    def gla_gates(self, h, qb, kb, rb, free):
        nc = self.nc
        f = free
        la = self.view(f, 4, 256)
        t = self.view(f + 1024, 4, 256)
        eb = self.view(f + 2048, 2, L)
        ab = self.cols(f + 3072, 512)
        wab = self.view(f + 3584, KD, 16)
        self.blast = self.view(f + 3712, 2, 8)
        kd = self.view(f, 2, L)
        self.gla_kd, self.gla_dec = kd, eb
        self.gla_q, self.gla_k = qb, kb
        sems = {n: self.sem("gla_" + n) for n in ["w", "one", "ab", "abk", "x", "lin", "abs", "ln", "la", "b", "eb", "nb",
                                                  "ld", "ed", "done", "er", "ner", "low", "t"]}
        s = sems
        flat = lambda a: a.rearrange("p a b -> p (a b)")
        xb = [self.bank[1 + j][:, :].rearrange("p (a b) -> p a b", a=2) for j in range(2)]
        with nc.Block() as block:
            @block.sync
            def _(sp):
                sp.dma_start(wab, self.ins["w_ab"].rearrange("p (k m) -> p k m", k=KD)).then_inc(s["w"], 16)

            @block.tensor
            def _(pe):
                pe.wait_ge(s["w"], 16)
                for k in range(KD):
                    mm = pe.matmul(self.bank[0][0:16, :], wab[:, k, :], h[:, k, :], start=(k == 0), stop=(k == KD - 1))
                mm.then_inc(s["ab"], 1)
                pe.wait_ge(s["abk"], 1)
                for b in range(4):
                    mm = pe.matmul(xb[b // 2][:, b % 2, :], ab[0:17, b * P:(b + 1) * P], self.S("gate_up")[0:17, :],
                                   start=True, stop=True)
                mm.then_inc(s["x"], 1)
                pe.wait_ge(s["la"], 1)
                for c in range(2):
                    for b in range(4):
                        mm = pe.matmul(self.bank[3 + c][:, b * P:(b + 1) * P], la[:, b, c * P:(c + 1) * P],
                                       self.C("tri64"), start=True, stop=True)
                mm.then_inc(s["b"], 1)

            @block.vector
            def _(dve):
                self.dve.after(dve, dve.memset(ab[0:17, :], 1.0))
                dve.wait_ge(s["ab"], 1)
                dve.tensor_copy(ab[0:16, :], self.bank[0][0:16, :]).then_inc(s["abk"], 1)
                dve.wait_ge(s["x"], 1)
                for j in range(2):
                    tj, lj = t[:, 2 * j:2 * j + 2, :], la[:, 2 * j:2 * j + 2, :]
                    dve.tensor_scalar(lj, xb[j], 0.0, None, ALU.min)
                    self.dve.after(dve, dve.tensor_scalar(tj, xb[j], 0.0, None, ALU.max))
                    last = dve.scalar_tensor_tensor(tj, tj, 2.0, xb[j], ALU.mult, ALU.subtract)
                last.then_inc(s["abs"], 1)
                dve.wait_ge(s["ln"], 1)
                self.dve.after(dve, dve.tensor_tensor(la, la, t, ALU.subtract))
                dve.tensor_scalar(la, la, 1.0 / 16.0, None, ALU.mult).then_inc(s["la"], 1)
                dve.wait_ge(s["eb"], 2)
                for c in range(2):
                    dve.scalar_tensor_tensor(qb[:, c, :], qb[:, c, :], 0.125, eb[:, c, :], ALU.mult, ALU.mult)
                b64 = [self.bank[3 + c][:, :].rearrange("p (n i) -> p n i", i=64) for c in range(2)]
                for c in range(2):
                    last = dve.tensor_copy(self.blast[:, c, :], b64[c][:, :, 63])
                self.dve.after(dve, last)
                for c in range(2):
                    last = dve.tensor_tensor(kd[:, c, :].rearrange("p (n i) -> p n i", i=64),
                                             self.blast[:, c, :].rearrange("p (n o) -> p n o", o=1).to_broadcast([P, 8, 64]),
                                             b64[c], ALU.subtract)
                last.then_inc(s["ld"], 1)
                dve.wait_ge(s["ed"], 1)
                self.dve.after(dve, dve.tensor_tensor(kd, kd, kb, ALU.mult))
                dve.tensor_tensor(kb, kb, flat2(t), ALU.mult)

            @block.scalar
            def _(act):
                act.activation(rb, rb, ACT.Silu)
                act.wait_ge(s["abs"], 1)
                self.act.after(act, act.activation(t, t, ACT.Exp, scale=-1.0))
                act.activation(t, t, ACT.Ln, bias=1.0).then_inc(s["ln"], 1)
                act.wait_ge(s["b"], 1)
                for c in range(2):
                    act.activation(eb[:, c, :], self.bank[3 + c][:, :], ACT.Exp)
                for c in range(2):
                    last = act.activation(flat2(t)[:, c, :], self.bank[3 + c][:, :], ACT.Exp, scale=-1.0)
                last.then_inc(s["eb"], 2)
                act.wait_ge(s["ld"], 1)
                act.activation(kd, kd, ACT.Exp).then_inc(s["ed"], 1)

    def swa(self, qa, ka, va, band, o, free):
        nc = self.nc
        f = free
        pbuf = self.view(f, H, 2 * P)
        pT = self.view(f + 2048, 2 * H, P)
        f += 4096
        small = lambda i: self.cols(f + 8 * i, 8)
        mx, negm, sm, es, rc = (small(i) for i in range(5))
        s = {n: self.sem("swa_" + n) for n in ["s", "lg", "m", "e", "es", "p", "t", "tk", "o", "ok", "band", "pm"]}
        sc = [self.bank[i][:, :].rearrange("p (a b) -> p a b", a=2) for i in range(4)]
        tb = [self.bank[4 + i][:, :].rearrange("p (a b) -> p a b", a=4) for i in range(2)]
        ob = [self.bank[6 + i][:, :].rearrange("p (a b) -> p a b", a=4) for i in range(2)]
        with nc.Block() as block:
            @block.tensor
            def _(pe):
                for n in range(4):
                    lo = 0 if n else P
                    if n >= 1:
                        pe.wait_ge(s["lg"], n)
                    for hh in range(H):
                        c, half = hh % 4, hh // 4
                        rows = slice(64 * half, 64 * half + 64)
                        mm = pe.matmul(sc[hh // 2][:, hh % 2, lo:], qa[rows, c, n * P:(n + 1) * P],
                                       ka[rows, 0, (n - 1) * P + lo:(n + 1) * P], start=True, stop=True)
                    mm.then_inc(s["s"], 1)
                    pe.wait_ge(s["p"], n + 1)
                    for q in range(4):
                        if 4 * n + q >= 2:
                            pe.wait_ge(s["tk"], 4 * n + q - 1)
                        for i in range(4):
                            if i % 2 == 0 and n == 0:
                                continue
                            mm = pe.transpose(tb[q % 2][:, i, :], pbuf[:, 2 * q + i // 2, (i % 2) * P:(i % 2 + 1) * P],
                                              self.C("ident"))
                        mm.then_inc(s["t"], 1)
                    pe.wait_ge(s["tk"], 4 * n + 4)
                    if n >= 1:
                        pe.wait_ge(s["ok"], n)
                    for hh in range(H):
                        for i in range(2) if n else [1]:
                            mm = pe.matmul(ob[hh // 4][:, hh % 4, :], va[:, n - 1 + i, :], pT[:, 2 * hh + i, :],
                                           start=(i == (0 if n else 1)), stop=(i == 1))
                    mm.then_inc(s["o"], 1)

            @block.gpsimd
            def _(pool):
                pool.tensor_tensor(self.swa_band, band,
                                   self.C("swa").rearrange("p (a b) -> p a b", a=1).to_broadcast([P, H, 2 * P]),
                                   ALU.add).then_inc(s["band"], 1)
                for n in range(4):
                    lo = 0 if n else P
                    pool.wait_ge(s["pm"], n + 1)
                    w = 2 * P - lo
                    pool.tensor_tensor(pbuf[:, :, lo:], pbuf[:, :, lo:],
                                       rc.rearrange("p (a o) -> p a o", o=1).to_broadcast([P, H, w]), ALU.mult).then_inc(s["p"], 1)

            @block.vector
            def _(dve):
                dve.wait_ge(s["band"], 1)
                for n in range(4):
                    lo = 0 if n else P
                    dve.wait_ge(s["s"], n + 1)
                    if n >= 1:
                        dve.wait_ge(s["t"], 4 * n)
                    for q in range(4):
                        last = dve.scalar_tensor_tensor(pbuf[:, 2 * q:2 * q + 2, lo:], sc[q][:, :, lo:], 0.125,
                                                        self.swa_band[:, 2 * q:2 * q + 2, lo:], ALU.mult, ALU.add)
                    last.then_inc(s["lg"], 1)
                    dve.wait_ge(s["lg"], n + 1)
                    self.dve.after(dve, dve.tensor_reduce(mx, pbuf[:, :, lo:], AX.X, ALU.max))
                    self.dve.after(dve, dve.tensor_tensor(mx, mx, self.S("sinks"), ALU.max))
                    dve.tensor_tensor(es, self.S("sinks"), mx, ALU.subtract)
                    dve.tensor_scalar(negm, mx, -1.0, None, ALU.mult).then_inc(s["m"], 1)
                    dve.wait_ge(s["e"], n + 1)
                    self.dve.after(dve, dve.tensor_tensor(sm, sm, es, ALU.add))
                    dve.reciprocal(rc, sm).then_inc(s["pm"], 1)
                    for q in range(4):
                        dve.wait_ge(s["t"], 4 * n + q + 1)
                        i0 = 0 if n else 1
                        dve.tensor_copy(pT[:, 4 * q + i0:4 * q + 4:1 if n else 2, :], tb[q % 2][:, i0::1 if n else 2, :]).then_inc(s["tk"], 1)
                    dve.wait_ge(s["o"], n + 1)
                    dve.tensor_copy(o[0:64, 0:4, n * P:(n + 1) * P], ob[0][0:64, :, :])
                    dve.tensor_copy(o[64:128, 0:4, n * P:(n + 1) * P], ob[1][64:128, :, :]).then_inc(s["ok"], 1)

            @block.scalar
            def _(act):
                for n in range(4):
                    lo = 0 if n else P
                    act.wait_ge(s["m"], n + 1)
                    act.activation(es, es, ACT.Exp)
                    for hh in range(H):
                        last = act.activation(pbuf[:, hh, lo:], pbuf[:, hh, lo:], ACT.Exp, bias=negm[:, hh:hh + 1],
                                              accum_out=sm[:, hh:hh + 1])
                    last.then_inc(s["e"], 1)

    def gla(self, vb, o, free):
        nc = self.nc
        kd, dec, qd, kn = self.gla_kd, self.gla_dec, self.gla_q, self.gla_k
        f = free + 3072
        att = [[self.view(f + 512 * i + 256 * half, 2, P) for half in range(2)] for i in range(2)]
        kdn = [self.view(f + 1024 + 256 * i, 2, P) for i in range(2)]
        St = self.view(f + 1536, 2, P)
        s = {n: self.sem("gla_" + n) for n in ["zero", "att", "attk", "kt", "kk", "o", "ok", "u", "st"]}
        pair = lambda i: self.bank[i][:, 0:256].rearrange("p (a b) -> p a b", a=2)
        rows = [slice(0, 64), slice(64, 128)]
        with nc.Block() as block:
            @block.tensor
            def _(pe):
                pe.wait_ge(s["zero"], 1)
                for b in range(4):
                    cols = slice(b * P, (b + 1) * P)
                    if b >= 1:
                        pe.wait_ge(s["kk"], b)
                    for half in range(2):
                        for c in range(2):
                            mm = pe.matmul(pair(half)[:, c, :], kn[rows[half], c, cols], qd[rows[half], c, cols],
                                           start=True, stop=True)
                    mm.then_inc(s["att"], 1)
                    for c in range(2):
                        mm = pe.transpose(pair(2)[:, c, :], kd[:, c, cols], self.C("ident"))
                    mm.then_inc(s["kt"], 1)
                    pe.wait_ge(s["attk"], b + 1)
                    pe.wait_ge(s["kk"], b + 1)
                    if b >= 1:
                        pe.wait_ge(s["ok"], b)
                    for cc in range(2):
                        n = 2 * b + cc
                        if n >= 1:
                            pe.wait_ge(s["st"], n)
                        part = slice(64 * cc, 64 * cc + 64)
                        tok = slice(b * P + 64 * cc, b * P + 64 * cc + 64)
                        for half in range(2):
                            for c in range(2):
                                hh = 2 * c + half
                                out = pair(3 + half)[:, c, part]
                                pe.matmul(out, vb[:, b, hh * P:(hh + 1) * P], att[b % 2][half][:, c, part],
                                          start=True, stop=False)
                                mm = pe.matmul(out, St[rows[half], c, :], qd[rows[half], c, tok], start=False, stop=True)
                        mm.then_inc(s["o"], 1)
                        for c in range(2):
                            mm = pe.matmul(self.bank[6 + n % 2][:, c * 256:c * 256 + 256], kdn[b % 2][part, c, :],
                                           vb[part, b, c * 256:c * 256 + 256], start=True, stop=True)
                        mm.then_inc(s["u"], 1)

            @block.vector
            def _(dve):
                dve.memset(St, 0.0).then_inc(s["zero"], 1)
                tri = self.C("tri64").rearrange("p (a b) -> p a b", a=1).to_broadcast([P, 2, P])
                for b in range(4):
                    dve.wait_ge(s["att"], b + 1)
                    for half in range(2):
                        last = dve.tensor_tensor(att[b % 2][half], pair(half), tri, ALU.mult)
                    last.then_inc(s["attk"], 1)
                    dve.wait_ge(s["kt"], b + 1)
                    dve.tensor_copy(kdn[b % 2], pair(2)).then_inc(s["kk"], 1)
                    for cc in range(2):
                        n = 2 * b + cc
                        dve.wait_ge(s["u"], n + 1)
                        if n >= 1:
                            dve.wait_ge(s["st"], n)
                        else:
                            dve.wait_ge(s["zero"], 1)
                        for hh in range(4):
                            r = rows[hh % 2]
                            last = dve.scalar_tensor_tensor(
                                St[r, hh // 2, :], St[r, hh // 2, :], dec[r, hh // 2, 64 * n + 63:64 * n + 64],
                                self.bank[6 + n % 2][r, hh * P:(hh + 1) * P], ALU.mult, ALU.add)
                        last.then_inc(s["st"], 1)

            @block.scalar
            def _(act):
                for b in range(4):
                    act.wait_ge(s["o"], 2 * b + 2)
                    for half in range(2):
                        last = act.activation(o[:, 4 + half:8:2, b * P:(b + 1) * P], pair(3 + half), ACT.Copy)
                    last.then_inc(s["ok"], 1)

    def odd_mixer(self):
        f = self.free0
        h = self.view(f, KD, L)
        o = h
        q, k, vT = self.view(f + 4096, H, L), self.view(f + 8192, H, L), self.view(f + 12288, H, L)
        v = self.view(f + 16384, 4, H * P)
        band = self.view(f + 20480, H, 2 * P)
        free = f + 20480 + 2048
        self.project_all("odd", TILE0["odd_in"], [a[:, i, :] for a in (q, k, vT) for i in range(H)], h)
        self.turn_all("odd_v", [([vT[:, 4 * g + i, b * P:(b + 1) * P] for i in range(4)],
                                 v[:, b, 512 * g:512 * g + 512].rearrange("p (a b) -> p a b", a=4))
                                for b in range(4) for g in range(2)])
        self.head_norms("c_qk", [(q[:, i, :], self.S("c_q"), None) for i in range(H)] +
                        [(k[:, i, :], self.S("c_k"), None) for i in range(H)], "ones", P, free)
        self.swa_band = self.view(free + 2624, H, 2 * P)
        self.band_bias(band, self.swa_band)
        self.causal(q, k, v, band, o, free)
        self.project_out("odd_out", TILE0["odd_out"], o, self.mod["odd"][:, 16:24])

    def causal(self, q, k, v, band, o, free):
        nc = self.nc
        pb = [self.cols(free + 512 * i, 512) for i in range(3)]
        pT = [self.view(free + 1536 + 512 * i, 4, P) for i in range(2)]
        st = self.view(free + 2560, 4, 8)
        units = [(n, hh) for n in range(4) for hh in range(H)]
        N = len(units)
        s = {n: self.sem("moba_" + n) for n in ["band", "s", "lg", "m", "e", "p", "t", "tk", "o", "ok"]}
        far = self.cols(free + 2600, 8)

        def width(n):
            return (n + 1) * P

        with nc.Block() as block:
            @block.gpsimd
            def _(pool):
                pool.tensor_copy(far, band[:, :, 0])
                pool.tensor_tensor(self.swa_band, band, self.C("causal").rearrange("p (a b) -> p a b", a=1).to_broadcast([P, H, 2 * P]),
                                   ALU.add).then_inc(s["band"], 1)

            @block.tensor
            def _(pe):
                def turn(j):
                    n, hh = units[j]
                    pe.wait_ge(s["p"], j + 1)
                    if j >= 2:
                        pe.wait_ge(s["tk"], j - 1)
                    for i in range(n + 1):
                        mm = pe.transpose(self.bank[3 + j % 2][:, i * P:(i + 1) * P], pb[j % 3][:, i * P:(i + 1) * P], self.C("ident"))
                    mm.then_inc(s["t"], 1)

                def value(j):
                    n, hh = units[j]
                    pe.wait_ge(s["tk"], j + 1)
                    if j >= 8 and j % 4 == 0:
                        pe.wait_ge(s["ok"], j // 4 - 1)
                    for i in range(n + 1):
                        mm = pe.matmul(self.bank[5 + j // 4 % 2][:, (j % 4) * P:(j % 4 + 1) * P], v[:, i, hh * P:(hh + 1) * P],
                                       pT[j % 2][:, i, :], start=(i == 0), stop=(i == n))
                    mm.then_inc(s["o"], 1)

                for j, (n, hh) in enumerate(units):
                    if j >= 3:
                        pe.wait_ge(s["lg"], j - 2)
                    pe.matmul(self.bank[j % 3][:, 0:width(n)], q[:, hh, n * P:(n + 1) * P], k[:, hh, 0:width(n)],
                              start=True, stop=True).then_inc(s["s"], 1)
                    if j >= 2:
                        turn(j - 2)
                    if j >= 3:
                        value(j - 3)
                turn(N - 2)
                value(N - 3)
                turn(N - 1)
                value(N - 2)
                value(N - 1)

            @block.vector
            def _(dve):
                def keep(j):
                    n, hh = units[j]
                    dve.wait_ge(s["t"], j + 1)
                    if j >= 2:
                        dve.wait_ge(s["o"], j - 1)
                    dve.tensor_copy(pT[j % 2][:, 0:n + 1, :],
                                    self.bank[3 + j % 2][:, 0:width(n)].rearrange("p (a b) -> p a b", b=P)).then_inc(s["tk"], 1)

                def scale(j):
                    n, hh = units[j]
                    x = pb[j % 3][:, 0:width(n)]
                    c = st[:, 1, j % 4:j % 4 + 1]
                    dve.wait_ge(s["e"], j + 1)
                    self.dve.after(dve, dve.reciprocal(c, st[:, 2, j % 4:j % 4 + 1]))
                    dve.tensor_scalar(x, x, c, None, ALU.mult).then_inc(s["p"], 1)

                dve.wait_ge(s["band"], 1)
                for j, (n, hh) in enumerate(units):
                    dve.wait_ge(s["s"], j + 1)
                    if j >= 3:
                        dve.wait_ge(s["t"], j - 2)
                    x, b, w = pb[j % 3], self.bank[j % 3], width(n)
                    near = min(w, 2 * P)
                    if n >= 2:
                        dve.tensor_scalar(x[:, 0:w - near], b[:, 0:w - near], P ** -0.5, far[:, hh:hh + 1], ALU.mult, ALU.add)
                    last = dve.scalar_tensor_tensor(x[:, w - near:w], b[:, w - near:w], P ** -0.5,
                                                    self.swa_band[:, hh, 2 * P - near:], ALU.mult, ALU.add)
                    last.then_inc(s["lg"], 1)
                    dve.wait_ge(s["lg"], j + 1)
                    m = st[:, 0, j % 4:j % 4 + 1]
                    self.dve.after(dve, dve.tensor_reduce(m, x[:, 0:w], AX.X, ALU.max))
                    dve.tensor_scalar(st[:, 3, j % 4:j % 4 + 1], m, -1.0, None, ALU.mult).then_inc(s["m"], 1)
                    if j >= 1:
                        scale(j - 1)
                    if j >= 2:
                        keep(j - 2)
                scale(N - 1)
                keep(N - 2)
                keep(N - 1)

            @block.scalar
            def _(act):
                def out(g):
                    n, hh = units[4 * g]
                    act.wait_ge(s["o"], 4 * g + 4)
                    act.activation(o[:, hh:hh + 4, n * P:(n + 1) * P],
                                   self.bank[5 + g % 2][:, :].rearrange("p (a b) -> p a b", a=4), ACT.Copy).then_inc(s["ok"], 1)

                for j, (n, hh) in enumerate(units):
                    act.wait_ge(s["m"], j + 1)
                    x = pb[j % 3][:, 0:width(n)]
                    act.activation(x, x, ACT.Exp, bias=st[:, 3, j % 4:j % 4 + 1],
                                   accum_out=st[:, 2, j % 4:j % 4 + 1]).then_inc(s["e"], 1)
                    if j % 4 == 3 and j >= 7:
                        out(j // 4 - 1)
                out(N // 4 - 1)

    def load_context(self):
        nc, loaded = self.nc, self.sem("context_loaded")
        xc = self.view(self.free0 + KD * (L + LC), KD, LC)
        with nc.Block() as block:
            @block.sync
            def _(sp):
                sp.dma_start(xc, self.ins["ctxT"].rearrange("p (k t) -> p k t", k=KD)).then_inc(loaded, 16)
                sp.wait_ge(loaded, 16)
        return xc

    def route(self, layer):
        nc = self.nc
        f = self.free0
        h = self.view(f, KD, L)
        rows = self.view(f + 4096, 4, D)
        f += 8192
        wr = self.view(f, KD, 36)
        f += 288
        at = [f]

        def new(a, b):
            v = self.view(at[0], a, b)
            at[0] += a * b
            return v

        lg, gl, gm, ge, gs = new(4, 36), new(4, 4), new(4, 1), new(4, 4), new(4, 1)
        gsel, em, masked = new(4, 1), new(4, 32), new(4, 32)
        t32, oh = new(4, 32), [new(4, 32), new(4, 32)]
        v1, v2, idx = new(4, 1), new(4, 1), new(8, 1)
        oh12, cnt, ov, oe = new(4, 32), new(1, 32), new(1, 32), new(1, 32)
        rank, pm, ps, blk, st = new(8, 1), new(8, 1), new(8, 1), new(8, 1), new(8, 1)
        A, B = new(8, P), new(8, BLOCKS)
        le = new(8, 32)
        k0 = self.total - 128
        self.slot_tok = self.cols(k0, BLOCKS).bitcast(U32)
        self.pair_slot = self.cols(k0 + 40, 8).bitcast(U32)
        self.weight = self.view(k0 + 48, 8, 1)
        self.spare = self.cols(k0 + 56, 8).bitcast(I32)
        spare_f = self.cols(k0 + 64, 8)
        s = {n: self.sem("route_" + n) for n in ["w", "lg", "turned", "kept", "stored", "e", "ex", "oh", "rank", "ab", "tok"]}
        c3 = lambda n, a: self.C(n).rearrange("p (a b) -> p a b", a=1).to_broadcast([P, a, COL[n][1]])
        bias = self.S("moe_b", 36 * layer, 36 * layer + 36).rearrange("p (a b) -> p a b", a=1).to_broadcast([P, 4, 36])
        with nc.Block() as block:
            @block.sync
            def _(sp):
                sp.dma_start(wr, self.ins["w_route"][layer].rearrange("p (k m) -> p k m", k=KD)).then_inc(s["w"], 16)
                for b in range(4):
                    sp.wait_ge(s["kept"], 2 * b + 2)
                    sp.dma_start(self.rows[b * P:(b + 1) * P, :], rows[:, b, :]).then_inc(s["stored"], 16)
                sp.wait_ge(s["stored"], 64)

            @block.tensor
            def _(pe):
                pe.wait_ge(s["w"], 16)
                for b in range(4):
                    for k in range(KD):
                        mm = pe.matmul(self.bank[0][:, b * 36:b * 36 + 36], h[:, k, b * P:(b + 1) * P], wr[:, k, :],
                                       start=(k == 0), stop=(k == KD - 1))
                mm.then_inc(s["lg"], 1)
                for n in range(8):
                    if n >= 2:
                        pe.wait_ge(s["kept"], n - 1)
                    for i in range(4):
                        mm = pe.transpose(self.bank[1 + n % 2][:, i * P:(i + 1) * P],
                                          h[:, 4 * (n % 2) + i, (n // 2) * P:(n // 2 + 1) * P], self.C("ident"))
                    mm.then_inc(s["turned"], 1)
                pe.wait_ge(s["oh"], 1)
                for b in range(4):
                    for a in range(b):
                        pe.matmul(self.bank[3][:, b * 32:b * 32 + 32], self.C("ones"), oh12[:, a, :], start=(a == 0), stop=False)
                    pe.matmul(self.bank[3][:, b * 32:b * 32 + 32], self.C("stri"), oh12[:, b, :], start=(b == 0), stop=True)
                for b in range(4):
                    mm = pe.matmul(self.bank[3][:, 128:160], self.C("ones"), oh12[:, b, :], start=(b == 0), stop=(b == 3))
                mm.then_inc(s["rank"], 1)
                pe.wait_ge(s["ab"], 1)
                for j in range(8):
                    mm = pe.matmul(self.bank[4][:, 0:BLOCKS], A[:, j, :], B[:, j, :], start=(j == 0), stop=(j == 7))
                mm.then_inc(s["tok"], 1)

            @block.scalar
            def _(act):
                for n in range(8):
                    act.wait_ge(s["turned"], n + 1)
                    act.activation(rows[:, n // 2, 512 * (n % 2):512 * (n % 2) + 512], self.bank[1 + n % 2][:, :],
                                   ACT.Copy).then_inc(s["kept"], 1)
                act.wait_ge(s["e"], 1)
                act.activation(ge, ge, ACT.Exp).then_inc(s["ex"], 1)
                act.wait_ge(s["e"], 2)
                act.activation(v2, v2, ACT.Exp).then_inc(s["ex"], 1)

            @block.vector
            def _(dve):
                def do(ins):
                    self.dve.after(dve, ins)

                def wide(a, n):
                    return a.to_broadcast([P, a.shape[1], n])

                def first_best(out, x, best, tmp, iota):
                    do(dve.tensor_reduce(best, x, AX.X, ALU.max))
                    do(dve.tensor_tensor(tmp, x, wide(best, x.shape[2]), ALU.is_equal))
                    do(dve.scalar_tensor_tensor(tmp, tmp, -100.0, iota, ALU.mult, ALU.add))
                    do(dve.tensor_reduce(out, tmp, AX.X, ALU.min))
                    do(dve.tensor_scalar(out, out, 100.0, None, ALU.add))

                dve.wait_ge(s["lg"], 1)
                do(dve.tensor_tensor(lg, self.bank[0][:, 0:144].rearrange("p (a b) -> p a b", a=4), bias, ALU.add))
                first_best(gsel, lg[:, :, 0:4], gm, gl, c3("iota_g", 4))
                dve.tensor_tensor(ge, lg[:, :, 0:4], wide(gm, 4), ALU.subtract).then_inc(s["e"], 1)
                do(dve.tensor_tensor(em, c3("grp", 4), wide(gsel, 32), ALU.is_equal))
                dve.tensor_scalar(t32, em, 1e30, -1e30, ALU.mult, ALU.add)
                do(dve.tensor_tensor(masked, lg[:, :, 4:36], em, ALU.mult))
                do(dve.tensor_tensor(masked, masked, t32, ALU.add))
                first_best(idx[:, 0:4, :], masked, v1, t32, c3("iota_e", 4))
                do(dve.tensor_tensor(oh[0], c3("iota_e", 4), wide(idx[:, 0:4, :], 32), ALU.is_equal))
                do(dve.scalar_tensor_tensor(masked, oh[0], -2e30, masked, ALU.mult, ALU.add))
                first_best(idx[:, 4:8, :], masked, v2, t32, c3("iota_e", 4))
                do(dve.tensor_tensor(oh[1], c3("iota_e", 4), wide(idx[:, 4:8, :], 32), ALU.is_equal))
                dve.tensor_tensor(oh12, oh[0], oh[1], ALU.add).then_inc(s["oh"], 1)
                dve.tensor_tensor(v2, v2, v1, ALU.subtract).then_inc(s["e"], 1)
                dve.wait_ge(s["ex"], 2)
                do(dve.tensor_reduce(gs, ge, AX.X, ALU.add))
                do(dve.scalar_tensor_tensor(gs, v2, 1.0, gs, ALU.add, ALU.mult))
                do(dve.reciprocal(self.weight[:, 0:4, :], gs))
                do(dve.tensor_tensor(self.weight[:, 4:8, :], self.weight[:, 0:4, :], v2, ALU.mult))
                dve.wait_ge(s["rank"], 1)
                rk = self.bank[3][:, 0:128].rearrange("p (a b) -> p a b", a=4)
                for j in range(2):
                    do(dve.tensor_tensor(t32, oh[j], rk, ALU.mult))
                    do(dve.tensor_reduce(rank[:, 4 * j:4 * j + 4, :], t32, AX.X, ALU.add))
                c2 = self.bank[3][:, 128:160]
                cn, o2, e2 = (x.rearrange("p a b -> p (a b)") for x in (cnt, ov, oe))
                do(dve.tensor_copy(cn, c2))
                do(dve.tensor_scalar(o2, cn, 128.5, None, ALU.is_gt))
                do(dve.scalar_tensor_tensor(o2, cn, 256.5, o2, ALU.is_gt, ALU.add))
                do(dve.scalar_tensor_tensor(o2, cn, 384.5, o2, ALU.is_gt, ALU.add))
                do(dve.tensor_tensor_scan(e2, self.C("ones")[:, 0:32], o2, 0.0, ALU.mult, ALU.add))
                do(dve.tensor_tensor(le, oe.to_broadcast([P, 8, 32]),
                                     self.C("blk").rearrange("p (a b) -> p a b", b=1).to_broadcast([P, 8, 32]), ALU.is_le))
                do(dve.tensor_reduce(spare_f, le, AX.X, ALU.add))
                do(dve.tensor_scalar(spare_f, spare_f, 31.0, None, ALU.min))
                do(dve.tensor_copy(spare_f[:, OVF:OVF + 1], e2[:, NE - 1:NE]))
                do(dve.tensor_copy(self.spare, spare_f))
                do(dve.tensor_tensor(o2, e2, o2, ALU.subtract))
                for j in range(2):
                    do(dve.tensor_tensor(t32, oh[j], ov.to_broadcast([P, 4, 32]), ALU.mult))
                    do(dve.tensor_reduce(st[:, 4 * j:4 * j + 4, :], t32, AX.X, ALU.add))
                do(dve.tensor_scalar(pm, rank, 127.5, None, ALU.is_gt))
                do(dve.tensor_copy(ps, pm))
                do(dve.scalar_tensor_tensor(pm, rank, 255.5, pm, ALU.is_gt, ALU.add))
                do(dve.scalar_tensor_tensor(pm, rank, 383.5, pm, ALU.is_gt, ALU.add))
                do(dve.tensor_tensor(st, st, pm, ALU.add))
                do(dve.tensor_tensor(st, st, idx, ALU.subtract))
                do(dve.scalar_tensor_tensor(st, st, 31.0, ps, ALU.add, ALU.mult))
                do(dve.tensor_tensor(blk, idx, st, ALU.add))
                do(dve.scalar_tensor_tensor(pm, pm, -128.0, rank, ALU.mult, ALU.add))
                do(dve.tensor_tensor(A, c3("iota", 8), wide(pm, P), ALU.is_equal))
                i39 = self.C("iota")[:, 0:BLOCKS].rearrange("p (a b) -> p a b", a=1).to_broadcast([P, 8, BLOCKS])
                do(dve.tensor_tensor(B, i39, wide(blk, BLOCKS), ALU.is_equal))
                tok = self.C("tok").rearrange("p (a b) -> p a b", b=1).to_broadcast([P, 4, BLOCKS])
                dve.tensor_tensor(B[:, 0:4, :], B[:, 0:4, :], tok, ALU.mult)
                dve.tensor_tensor(B[:, 4:8, :], B[:, 4:8, :], tok, ALU.mult).then_inc(s["ab"], 1)
                do(dve.scalar_tensor_tensor(st, blk, 128.0, pm, ALU.mult, ALU.add))
                dve.tensor_copy(self.pair_slot, st.rearrange("p a b -> p (a b)"))
                dve.wait_ge(s["tok"], 1)
                dve.tensor_copy(self.slot_tok, self.bank[4][:, 0:BLOCKS])

    def blank_spare_rows(self, eng, zeros, sem):
        for b in range(NE, BLOCKS):
            eng.dma_start(self.yrows[b * P:(b + 1) * P, :].rearrange("p (a b) -> p a b", a=2), zeros).then_inc(sem, 16)

    def experts(self, layer):
        self.expert_blocks(layer, "moe_", 0, NE)
        self.expert_blocks(layer, f"moe_spare{layer}_", NE, OVF)

    def expert_blocks(self, layer, name, b0, B):
        nc, spare = self.nc, b0 > 0
        f = self.free0
        w13 = [self.view(f + 8192 * i, 16, EH) for i in range(2)]
        f += 16384
        w2 = [self.view(f + 4096 * i, 4, D) for i in range(2)]
        f += 8192
        xr = [self.cols(f + 1024 * i, D) for i in range(2)]
        xT = self.view(f + 2048, KD, P)
        y = [self.cols(f + 3072 + 1024 * i, D) for i in range(2)]
        a = [self.cols(f + 5632 + 512 * i, EH) for i in range(2)]
        aT = self.view(f + 6656, 4, P)
        assert f + 7168 <= self.total - 128
        s = {n: self.sem(name + n) for n in ["turned", "kept0", "kept1", "h1", "h3", "silu", "a", "aturned", "akept", "y", "yk0", "yk1"]}
        w13_in, w2_in = [[self.sem(f"{name}{n}_loaded{i}") for i in range(2)] for n in ("w13", "w2")]
        x_in = [self.software_sem(f"{name}rows_gathered{i}") for i in range(2)]
        x_in_before = 0 if spare else 16 * layer * (B // 2)
        y_out = [self.sem(f"{name}y_stored{i}") for i in range(2)]
        W13, W2 = self.ins["w13"][layer], self.ins["w2"][layer]
        nth = lambda b: 16 * (b // 2 + 1)

        def sync_steps(sp):
            for b in range(B):
                if spare:
                    ex = sp.value_load(self.spare[0:1, b:b + 1], min_val=0, max_val=NE - 1)
                if b >= 2:
                    sp.wait_ge(s["h3"], b - 1)
                src = W13[b] if not spare else W13[bass.ds(ex, 1)].rearrange("a p n -> (a p) n")
                sp.dma_start(w13[b % 2], src.rearrange("p (k n) -> p k n", k=16)).then_inc(w13_in[b % 2], 16)
                if b >= 2:
                    sp.wait_ge(s["y"], b - 1)
                src = W2[b] if not spare else W2[bass.ds(ex, 1)].rearrange("a p n -> (a p) n")
                sp.dma_start(w2[b % 2], src.rearrange("p (k n) -> p k n", k=4)).then_inc(w2_in[b % 2], 16)

        def gpsimd_steps(pool):
            for b in range(B):
                if b >= 2:
                    pool.wait_ge(s["turned"], b - 1)
                pool.indirect_dma_start(xr[b % 2], None, self.rows[:, :],
                                        bass.IndirectOffsetOnAxis(self.slot_tok[:, b0 + b:b0 + b + 1], 0)).then_inc(x_in[b % 2], 16)

        def tensor_steps(pe):
            def hidden(b):
                pe.wait_ge(x_in[b % 2], x_in_before + nth(b))
                if b >= 1:
                    pe.wait_ge(s["kept0"], b)
                    pe.wait_ge(s["kept1"], b)
                for k in range(KD):
                    mm = pe.transpose(self.bank[k // 4][:, k % 4 * P:(k % 4 + 1) * P], xr[b % 2][:, k * P:(k + 1) * P],
                                      self.C("ident"))
                mm.then_inc(s["turned"], 1)
                pe.wait_ge(s["kept0"], b + 1)
                pe.wait_ge(s["kept1"], b + 1)
                pe.wait_ge(w13_in[b % 2], nth(b))
                if b >= 2:
                    pe.wait_ge(s["a"], b - 1)
                for i, sem in enumerate([s["h1"], s["h3"]]):
                    for k in range(KD):
                        mm = pe.matmul(self.bank[2 + 2 * (b % 2) + i][:, :], xT[:, k, :], w13[b % 2][:, KD * i + k, :],
                                       start=(k == 0), stop=(k == KD - 1))
                    mm.then_inc(sem, 1)

            def output(b):
                pe.wait_ge(s["a"], b + 1)
                if b >= 1:
                    pe.wait_ge(s["yk0"], b)
                for k in range(4):
                    mm = pe.transpose(self.bank[6][:, k * P:(k + 1) * P], a[b % 2][:, k * P:(k + 1) * P], self.C("ident"))
                mm.then_inc(s["aturned"], 1)
                pe.wait_ge(s["akept"], b + 1)
                pe.wait_ge(w2_in[b % 2], nth(b))
                if b >= 1:
                    pe.wait_ge(s["yk1"], b)
                for i in range(2):
                    for k in range(4):
                        mm = pe.matmul(self.bank[7 - i][:, :], aT[:, k, :], w2[b % 2][:, k, 512 * i:512 * i + 512],
                                       start=(k == 0), stop=(k == 3))
                mm.then_inc(s["y"], 1)

            hidden(0)
            for b in range(B):
                if b + 1 < B:
                    hidden(b + 1)
                output(b)

        def scalar_steps(act):
            for b in range(B + 1):
                if b < B:
                    act.wait_ge(s["turned"], b + 1)
                    act.activation(xT[:, 0:4, :], self.bank[0][:, :].rearrange("p (a b) -> p a b", a=4), ACT.Copy).then_inc(s["kept0"], 1)
                    act.wait_ge(s["h1"], b + 1)
                    if b >= 2:
                        act.wait_ge(s["aturned"], b - 1)
                    act.activation(a[b % 2], self.bank[2 + 2 * (b % 2)][:, :], ACT.Silu).then_inc(s["silu"], 1)
                if b >= 1:
                    c = b - 1
                    act.wait_ge(s["y"], c + 1)
                    if c >= 2:
                        act.wait_ge(y_out[c % 2], nth(c) - 16)
                    act.activation(y[c % 2][:, 0:512], self.bank[7][:, :], ACT.Copy).then_inc(s["yk1"], 1)
                    act.wait_ge(s["yk0"], c + 1)
                    act.wait_ge(s["yk1"], c + 1)
                    act.dma_start(self.yrows[(b0 + c) * P:(b0 + c + 1) * P, :], y[c % 2]).then_inc(y_out[c % 2], 16)
            for i in range(2):
                act.wait_ge(y_out[i], nth(B - 1 if (B - 1) % 2 == i else B - 2))

        def vector_steps(dve):
            def out(c):
                dve.wait_ge(s["y"], c + 1)
                if c >= 2:
                    dve.wait_ge(y_out[c % 2], nth(c) - 16)
                dve.tensor_copy(y[c % 2][:, 512:1024], self.bank[6][:, :]).then_inc(s["yk0"], 1)

            def aturn(c):
                dve.wait_ge(s["aturned"], c + 1)
                dve.tensor_copy(aT, self.bank[6][:, :].rearrange("p (a b) -> p a b", a=4)).then_inc(s["akept"], 1)

            for b in range(B):
                dve.wait_ge(s["turned"], b + 1)
                dve.tensor_copy(xT[:, 4:8, :], self.bank[1][:, :].rearrange("p (a b) -> p a b", a=4)).then_inc(s["kept1"], 1)
                if b >= 1:
                    aturn(b - 1)
                h3 = self.bank[3 + 2 * (b % 2)]
                dve.wait_ge(s["silu"], b + 1)
                dve.wait_ge(s["h3"], b + 1)
                dve.tensor_tensor(a[b % 2], a[b % 2], h3[:, :], ALU.mult).then_inc(s["a"], 1)
                if b >= 1:
                    out(b - 1)
            aturn(B - 1)
            out(B - 1)

        def run(eng, steps):
            if spare:
                with eng.If(eng.value_load(self.spare[0:1, OVF:OVF + 1], min_val=0, max_val=OVF) > 0):
                    steps(eng)
            else:
                steps(eng)

        with nc.Block() as block:
            @block.sync
            def _(sp):
                run(sp, sync_steps)

            @block.gpsimd
            def _(pool):
                run(pool, gpsimd_steps)

            @block.tensor
            def _(pe):
                run(pe, tensor_steps)

            @block.scalar
            def _(act):
                run(act, scalar_steps)

            @block.vector
            def _(dve):
                run(dve, vector_steps)

    def combine(self, layer, gate):
        nc = self.nc
        f = self.free0
        ys = [[self.cols(f + 4096 * j + 1024 * b, D) for b in range(4)] for j in range(2)]
        s = {n: self.sem("sum_" + n) for n in ["made", "turned"]}
        got = [self.software_sem(f"sum_gathered{j}") for j in range(2)]
        with nc.Block() as block:
            @block.gpsimd
            def _(pool):
                for b in range(4):
                    for j in range(2):
                        pool.indirect_dma_start(ys[j][b], None, self.yrows[:, :],
                                                bass.IndirectOffsetOnAxis(self.pair_slot[:, 4 * j + b:4 * j + b + 1], 0)
                                                ).then_inc(got[j], 16)

            @block.vector
            def _(dve):
                for j in range(2):
                    dve.wait_ge(got[j], 64 * (layer + 1))
                for b in range(4):
                    self.dve.after(dve, dve.tensor_scalar(ys[0][b], ys[0][b], self.weight[:, b, :], None, ALU.mult))
                    dve.scalar_tensor_tensor(ys[0][b], ys[1][b], self.weight[:, 4 + b, :], ys[0][b], ALU.mult, ALU.add
                                             ).then_inc(s["made"], 1)
                for k in range(KD):
                    dve.wait_ge(s["turned"], k + 1)
                    dve.scalar_tensor_tensor(self.x[:, k, :], self.bank[k][:, :], gate[:, k:k + 1], self.x[:, k, :],
                                             ALU.mult, ALU.add)

            @block.tensor
            def _(pe):
                pe.wait_ge(s["made"], 4)
                for k in range(KD):
                    for b in range(4):
                        mm = pe.transpose(self.bank[k][:, b * P:(b + 1) * P], ys[0][b][:, k * P:(k + 1) * P], self.C("ident"))
                    mm.then_inc(s["turned"], 1)

    def store(self):
        nc = self.nc
        stored = self.output_stored
        with nc.Block() as block:
            @block.sync
            def _(sp):
                sp.dma_start(self.out.rearrange("p (k t) -> p k t", k=KD), self.x).then_inc(stored, 16)
                sp.wait_ge(stored, 16)


def flat2(t):
    return t.rearrange("p (a c) b -> p a (c b)", a=2)


def build(nc, ins, out, stages=99):
    p = Program(nc, ins, out)
    h = p.view(p.free0, KD, L)
    p.load_inputs()
    p.modulations_1()
    p.gdn_layout()
    lat, ctx = p.mod["lat"], p.mod["ctx"]
    xc = p.load_context()
    p.norm("norm1", [(p.h, p.x, L, p.S("norm1_g"), lat[:, 8:16], lat[:, 0:8]),
                     (p.hc, xc, LC, p.S("norm1_g"), ctx[:, 8:16], ctx[:, 0:8])])
    p.gdn_project()
    p.gdn_prepare()
    p.gdn_core()
    p.gdn_finish()
    p.residuals += KD
    p.retire()
    if stages < 1:
        return p
    p.norm("norm2", [(h, p.x, L, p.S("norm2_g"), lat[:, 32:40], lat[:, 24:32])])
    p.ffn()
    p.norm("final", [(h, p.x, L, p.S("final_g"), None, None)], final=p.x)
    p.retire()
    if stages < 2:
        return p
    for layer, name in enumerate(["even", "odd"]):
        mod = p.mod[name]
        p.norm(name + "1", [(h, p.x, L, p.S("norm1_2", 8 * layer, 8 * layer + 8), mod[:, 8:16], mod[:, 0:8])])
        if layer == 0:
            p.even_mixer()
        else:
            p.odd_mixer()
        p.retire()
        if stages < 3 + 2 * layer:
            return p
        p.norm(name + "2", [(h, p.x, L, p.S("norm2_2", 8 * layer, 8 * layer + 8), mod[:, 32:40], mod[:, 24:32])])
        p.route(layer)
        p.experts(layer)
        p.combine(layer, mod[:, 40:48])
        p.retire()
        if stages < 4 + 2 * layer:
            return p
    return p


def kernel_tiles(w):
    k, m = w.shape
    return w.reshape(k // P, P, m // P, P).transpose(2, 1, 0, 3).reshape(m // P, P, k)


def columns(v):
    return v.reshape(-1, P).T


def lay_out(i):
    dense = []
    w_mod = kernel_tiles(i["w_mod"][0])
    dense.append(w_mod[:16])
    w = i["gdn_w_in"][0]
    dense.append(kernel_tiles(w[:, :4096]))
    dense += [w_mod[16:], kernel_tiles(i["ada_w_2"][0]), kernel_tiles(i["ada_w_2"][1])]
    dense.append(kernel_tiles(i["gdn_w_out"][0]))
    w_ba = w[:, 4096:].reshape(KD, P, 32).transpose(1, 0, 2).reshape(P, KD * 32)
    w = kernel_tiles(i["ffn_w_in"][0])
    dense.append(np.stack([w[:KF], w[KF:]], 1).reshape(2 * KF, P, D))
    dense.append(i["ffn_w_out"][0].reshape(KF, P, D))
    w = i["even_w_in_2"][0]
    qa = w[:, :512].reshape(D, 2, 4, 64).transpose(0, 2, 1, 3).reshape(D, 512)
    dense.append(kernel_tiles(np.concatenate([qa, w[:, 512:2304]], 1)))
    w_ab = w[:, 2304:].reshape(KD, P, 16).transpose(1, 0, 2).reshape(P, KD * 16)
    w = i["even_w_out_2"][0]
    wa = w[:512].reshape(2, 4, 64, D).transpose(1, 0, 2, 3).reshape(512, D)
    dense.append(kernel_tiles(np.concatenate([wa, w[512:]], 0)))
    dense += [kernel_tiles(i["odd_w_in_2"][0]), kernel_tiles(i["odd_w_out_2"][0])]
    dense = np.concatenate(dense, 0)
    assert dense.shape == (NTILES, P, D)

    def every(v):
        return np.tile(np.reshape(v, (1, -1)), (P, 1))

    def rows(v):
        return np.concatenate([v, np.zeros((P - v.shape[0], v.shape[1]), v.dtype)], 0)

    taps = lambda w, n: w.T.reshape(n, P, -1).transpose(1, 0, 2).reshape(P, -1)
    sm = {"c1": np.stack([columns(i["c"][0]), columns(i["c_ctx"])], 2).reshape(P, 16),
          "mod_b": np.concatenate([columns(i["b_mod"][0]), columns(i["ada_b_2"])], 1), "norm1_g": columns(i["norm1_g"][0]), "norm2_g": columns(i["norm2_g"][0]),
          "final_g": columns(i["final_norm_g"]), "conv5": taps(i["gdn_conv_w"][0], 24),
          "gdn_norm": columns(i["gdn_norm_g"][0]), "a_log": every(i["gdn_a_log"]), "dt": every(i["gdn_dt_bias"]),
          "fconv": taps(i["ffn_conv_w"][0], KF), "fconv_b": columns(i["ffn_conv_b"][0]), "c2": columns(i["c_2"][0]),
          "norm1_2": columns(i["norm1_w_2"]), "norm2_2": columns(i["norm2_w_2"]),
          "a_q": columns(np.tile(i["a_q_norm_2"][0], 2)), "a_k": columns(np.tile(i["a_k_norm_2"][0], 2)),
          "sinks": every(i["a_sinks_2"][0]), "b_norm": columns(i["b_out_norm_2"][0]),
          "c_q": columns(i["c_q_norm_2"][0]), "c_k": columns(i["c_k_norm_2"][0]),
          "moe_b": every(np.concatenate([i["moe_b_group_2"], i["moe_b_expert_2"]], 1)),
          "rel": rows(i["rel_bias_2"]),
          "gate_up": rows(np.concatenate([i["b_gate_up_2"][0], i["b_gate_bias_2"]], 0))}
    smalls = np.concatenate([sm[n] for n, _ in SMALLS], 1)
    assert smalls.shape == (P, NSMALL), smalls.shape
    transposed = lambda x: x.reshape(-1, KD, P).transpose(2, 1, 0).reshape(P, -1)
    inner = lambda w, k: w.reshape(2, NE, k, P, -1).transpose(0, 1, 3, 2, 4).reshape(2, NE, P, -1)
    w13 = np.concatenate([inner(i["moe_w1_2"], KD), inner(i["moe_w3_2"], KD)], 3)
    w2 = inner(i["moe_w2_2"], 4)
    wr = np.concatenate([i["moe_w_group_2"], i["moe_w_expert_2"]], 2)
    wr = wr.reshape(2, KD, P, 36).transpose(0, 2, 1, 3).reshape(2, P, KD * 36)
    out = {"consts": constant_tables(), "smalls": smalls, "xT": transposed(i["x"][0]), "ctxT": transposed(i["ctx"][0]),
           "dense": dense, "w_ba": w_ba, "w_ab": w_ab, "w13": w13, "w2": w2, "w_route": wr}
    return {n: np.ascontiguousarray(a) for n, a in out.items()}


def kernel(**inputs):
    import concourse.bacc as bacc
    from concourse.bass_utils import run_bass_kernel_spmd

    arrays = lay_out({n: np.asarray(a) for n, a in inputs.items()})
    nc = bacc.Bacc("TRN2", target_bir_lowering=False, num_devices=1)
    ins = {n: nc.dram_tensor("in_" + n, a.shape, mybir.dt.from_np(a.dtype), kind="ExternalInput").ap()
           for n, a in arrays.items()}
    out = nc.dram_tensor("out_xT", (P, KD * L), F32, kind="ExternalOutput").ap()
    build(nc, ins, out).store()
    result = run_bass_kernel_spmd(nc, [{"in_" + n: a for n, a in arrays.items()}], core_ids=[0])
    xT = np.asarray(result.results[0]["out_xT"])
    return xT.reshape(P, KD, L).transpose(2, 1, 0).reshape(1, L, D)
```
